# Optimizing a Trainium2 kernel written in Bass

```python
import math
import jax
import jax.numpy as jnp
from jax import lax
import numpy as np

D_MODEL = 2048
BATCH = 1
SEQ = 256
DEPTH = 1

N_META = 16
CHUNK = 64
HG_CHUNK = 16
LEAD_PAD = CHUNK - N_META
EPS = 1e-6
NEG = -1e30
LB_FLOOR = 1e-30

HG_HEADS = 4
HG_KDIM = 128
HG_VDIM = 128
HG_KEY = HG_HEADS * HG_KDIM
HG_WIDTH = HG_HEADS * HG_VDIM

ML_HEADS = 4
ML_QK = 64
ML_V = 128
ML_QK_W = ML_HEADS * ML_QK
ML_WIDTH = ML_HEADS * ML_V
GATE_CAP = 15.0

SSM_HEADS = 16
SSM_HEADDIM = 64
SSM_WIDTH = SSM_HEADS * SSM_HEADDIM
SSM_STATE = 128
SSM_GROUPS = 4
SSM_BC = SSM_GROUPS * SSM_STATE
CONV_W = 4
CONV_CH = SSM_WIDTH + 2 * SSM_BC

D_MIX = HG_WIDTH + ML_WIDTH + SSM_WIDTH
IN_SPLITS = (HG_KEY, HG_KEY, HG_WIDTH, HG_WIDTH,
             ML_QK_W, ML_QK_W, ML_WIDTH, ML_WIDTH, ML_HEADS, ML_HEADS,
             SSM_WIDTH, CONV_CH, SSM_HEADS)
D_IN = sum(IN_SPLITS)

N_GROUPS_MOE = 4
EXPERTS_PER_GROUP = 8
N_EXPERTS = N_GROUPS_MOE * EXPERTS_PER_GROUP
TOP_K = 2
D_EXPERT = 512
MOE_BLOCK = 128

kernel_name = 'hymba_hgrn2_mlstm_ssd_hmoe'

def rmsnorm(x, w):
    xf = x.astype(jnp.float32)
    y = xf * lax.rsqrt(jnp.mean(xf * xf, axis=-1, keepdims=True) + EPS)
    return (y * w.astype(jnp.float32)).astype(x.dtype)

def group_rmsnorm(y, w, groups):
    shape = y.shape
    yg = y.reshape(shape[:-1] + (groups, shape[-1] // groups))
    yg = yg * lax.rsqrt(jnp.mean(yg * yg, axis=-1, keepdims=True) + EPS)
    return yg.reshape(shape) * w

def softcap(t):
    return GATE_CAP * jnp.tanh(t / GATE_CAP)

def split_last(t, sizes):
    offsets = [int(o) for o in np.cumsum(sizes)[:-1]]
    return jnp.split(t, offsets, axis=-1)

def lead_pad(t, value=0.0):
    widths = [(0, 0)] * t.ndim
    widths[1] = (LEAD_PAD, 0)
    return jnp.pad(t, widths, constant_values=value)

def causal_mask(c):
    return jnp.tril(jnp.ones((c, c), dtype=bool))

def carry_linear_state(decay, local):
    def step(s, inp):
        a, u = inp
        return a * s + u, s
    _, prev = lax.scan(step, jnp.zeros_like(local[0]), (decay, local))
    return prev

def hgrn2_mixer(q, f_logit, inp, g, lower_bound, norm_w):
    b = q.shape[0]
    log_lb = jnp.log(jnp.maximum(lower_bound, LB_FLOOR))
    log_f = jnp.logaddexp(log_lb, jnp.log1p(-lower_bound) + jax.nn.log_sigmoid(f_logit))
    q = lead_pad(q * HG_KDIM ** -0.5)
    log_f = lead_pad(log_f)
    v = lead_pad(inp)
    k = -jnp.expm1(log_f)
    p = q.shape[1]
    nc = p // HG_CHUNK

    def chunks(t, dim):
        return t.reshape(b, nc, HG_CHUNK, HG_HEADS, dim).transpose(0, 3, 1, 2, 4)

    q, k, log_f, v = chunks(q, HG_KDIM), chunks(k, HG_KDIM), chunks(log_f, HG_KDIM), chunks(v, HG_VDIM)
    cum = jnp.cumsum(log_f, axis=3)
    rel = jnp.where(causal_mask(HG_CHUNK)[:, :, None],
                    cum[..., :, None, :] - cum[..., None, :, :], NEG)
    scores = jnp.einsum('bhntd,bhnsd,bhntsd->bhnts', q, k, jnp.exp(rel))
    o_intra = jnp.einsum('bhnts,bhnsv->bhntv', scores, v)
    last = cum[..., -1:, :]
    local = jnp.einsum('bhnsd,bhnsv->bhndv', k * jnp.exp(last - cum), v)
    decay = jnp.exp(last[..., 0, :])[..., None]
    prev = jnp.moveaxis(carry_linear_state(jnp.moveaxis(decay, 2, 0), jnp.moveaxis(local, 2, 0)), 0, 2)
    o_inter = jnp.einsum('bhntd,bhndv->bhntv', q * jnp.exp(cum), prev)
    o = (o_intra + o_inter).transpose(0, 2, 3, 1, 4).reshape(b, p, HG_WIDTH)[:, LEAD_PAD:]
    return group_rmsnorm(o, norm_w, HG_HEADS) * jax.nn.silu(g)

def mlstm_mixer(q, k, v, o_pre, i_pre, f_pre, b_i, b_f, norm_w):
    b = q.shape[0]
    log_i = softcap(i_pre + b_i)
    log_f = jax.nn.log_sigmoid(softcap(f_pre + b_f))
    q = lead_pad(q * ML_QK ** -0.5)
    k = lead_pad(k)
    v = lead_pad(v)
    log_f = lead_pad(log_f)
    log_i = lead_pad(log_i, NEG)
    p = q.shape[1]
    nc = p // CHUNK

    def chunks(t, dim):
        return t.reshape(b, nc, CHUNK, ML_HEADS, dim).transpose(0, 3, 1, 2, 4)

    def gate_chunks(t):
        return t.reshape(b, nc, CHUNK, ML_HEADS).transpose(0, 3, 1, 2)

    q, k, v = chunks(q, ML_QK), chunks(k, ML_QK), chunks(v, ML_V)
    log_f, log_i = gate_chunks(log_f), gate_chunks(log_i)
    cum = jnp.cumsum(log_f, axis=-1)
    intra = jnp.where(causal_mask(CHUNK),
                      cum[..., :, None] - cum[..., None, :] + log_i[..., None, :], NEG)
    to_end = cum[..., -1:] - cum + log_i
    m_loc = jnp.max(to_end, axis=-1)
    w_end = jnp.exp(to_end - m_loc[..., None])
    c_loc = jnp.einsum('bhns,bhnsd,bhnsv->bhndv', w_end, k, v)
    n_loc = jnp.einsum('bhns,bhnsd->bhnd', w_end, k)
    total = cum[..., -1]

    def step(carry, inp):
        c_st, n_st, m_st = carry
        tot, ml, cl, nl = inp
        m_new = jnp.maximum(tot + m_st, ml)
        a = jnp.exp(tot + m_st - m_new)
        s = jnp.exp(ml - m_new)
        c_new = a[..., None, None] * c_st + s[..., None, None] * cl
        n_new = a[..., None] * n_st + s[..., None] * nl
        return (c_new, n_new, m_new), (c_st, n_st, m_st)

    init = (jnp.zeros((b, ML_HEADS, ML_QK, ML_V), c_loc.dtype),
            jnp.zeros((b, ML_HEADS, ML_QK), c_loc.dtype),
            jnp.zeros((b, ML_HEADS), c_loc.dtype))
    xs = (jnp.moveaxis(total, 2, 0), jnp.moveaxis(m_loc, 2, 0),
          jnp.moveaxis(c_loc, 2, 0), jnp.moveaxis(n_loc, 2, 0))
    _, (c_prev, n_prev, m_prev) = lax.scan(step, init, xs)
    c_prev, n_prev, m_prev = jnp.moveaxis(c_prev, 0, 2), jnp.moveaxis(n_prev, 0, 2), jnp.moveaxis(m_prev, 0, 2)
    inter = cum + m_prev[..., None]
    m_t = jnp.maximum(inter, jnp.max(intra, axis=-1))
    w_inter = jnp.exp(inter - m_t)
    qk = jnp.einsum('bhntd,bhnsd->bhnts', q, k) * jnp.exp(intra - m_t[..., None])
    num = jnp.einsum('bhnts,bhnsv->bhntv', qk, v) + w_inter[..., None] * jnp.einsum('bhntd,bhndv->bhntv', q, c_prev)
    den = jnp.sum(qk, axis=-1) + w_inter * jnp.einsum('bhntd,bhnd->bhnt', q, n_prev)
    h = num / jnp.maximum(jnp.abs(den), jnp.exp(-m_t))[..., None]
    h = h.transpose(0, 2, 3, 1, 4).reshape(b, p, ML_WIDTH)[:, LEAD_PAD:]
    return group_rmsnorm(h, norm_w, ML_HEADS) * jax.nn.sigmoid(o_pre)

def causal_depthwise_conv(x, w):
    return lax.conv_general_dilated(x, w.astype(x.dtype)[:, None, :], window_strides=(1,),
                                    padding=[(CONV_W - 1, 0)],
                                    dimension_numbers=('NWC', 'WIO', 'NWC'),
                                    feature_group_count=x.shape[-1])

def mamba2_mixer(z, xbc, dt_pre, conv_w, conv_b, dt_bias, a_log, d_skip, norm_w):
    b = z.shape[0]
    hpg = SSM_HEADS // SSM_GROUPS
    xbc = jax.nn.silu(causal_depthwise_conv(xbc, conv_w) + conv_b)
    x, bm, cm = split_last(xbc, (SSM_WIDTH, SSM_BC, SSM_BC))
    dt = jax.nn.softplus(dt_pre + dt_bias)
    a = -jnp.exp(a_log)
    x, bm, cm, dt = lead_pad(x), lead_pad(bm), lead_pad(cm), lead_pad(dt)
    p = x.shape[1]
    nc = p // CHUNK
    x = x.reshape(b, nc, CHUNK, SSM_GROUPS, hpg, SSM_HEADDIM)
    dt = dt.reshape(b, nc, CHUNK, SSM_GROUPS, hpg)
    bm = bm.reshape(b, nc, CHUNK, SSM_GROUPS, SSM_STATE)
    cm = cm.reshape(b, nc, CHUNK, SSM_GROUPS, SSM_STATE)
    cum = jnp.cumsum(jnp.moveaxis(dt * a.reshape(SSM_GROUPS, hpg), 2, -1), axis=-1)
    xdt = x * dt[..., None]
    decay_in = jnp.exp(jnp.where(causal_mask(CHUNK), cum[..., :, None] - cum[..., None, :], NEG))
    cb = jnp.einsum('bntgk,bnsgk->bngts', cm, bm)
    y_diag = jnp.einsum('bngts,bnghts,bnsghp->bntghp', cb, decay_in, xdt)
    to_end = jnp.exp(cum[..., -1:] - cum)
    local = jnp.einsum('bnsgk,bnghs,bnsghp->bnghpk', bm, to_end, xdt)
    chunk_decay = jnp.exp(cum[..., -1])[..., None, None]
    prev = jnp.moveaxis(carry_linear_state(jnp.moveaxis(chunk_decay, 1, 0), jnp.moveaxis(local, 1, 0)), 0, 1)
    y_off = jnp.einsum('bntgk,bnght,bnghpk->bntghp', cm, jnp.exp(cum), prev)
    y = y_diag + y_off + x * d_skip.reshape(SSM_GROUPS, hpg)[..., None]
    y = y.reshape(b, p, SSM_WIDTH)[:, LEAD_PAD:]
    return group_rmsnorm(y * jax.nn.silu(z), norm_w, SSM_GROUPS)

def hierarchical_moe(u, w_group, b_group, w_router, b_router, w1, w3, w2):
    b, l, d = u.shape
    t = u.reshape(-1, d)
    n_tok = t.shape[0]
    g_prob = jax.nn.softmax((t @ w_group).astype(jnp.float32) + b_group, axis=-1)
    g_sel = jnp.argmax(g_prob, axis=-1)
    g_gate = jnp.max(g_prob, axis=-1)
    e_logits = jnp.einsum('td,gde->tge', t, w_router).astype(jnp.float32) + b_router
    e_logits = jnp.einsum('tg,tge->te', jax.nn.one_hot(g_sel, N_GROUPS_MOE, dtype=jnp.float32), e_logits)
    top_v, top_i = lax.top_k(e_logits, TOP_K)
    top_w = jax.nn.softmax(top_v, axis=-1) * g_gate[:, None]
    flat_e = (g_sel[:, None] * EXPERTS_PER_GROUP + top_i).reshape(-1).astype(jnp.int32)
    flat_w = top_w.reshape(-1)
    tk = flat_e.shape[0]
    order = jnp.argsort(flat_e).astype(jnp.int32)
    sorted_e = flat_e[order]
    counts = jnp.bincount(flat_e, length=N_EXPERTS).astype(jnp.int32)
    starts = jnp.cumsum(counts) - counts
    padded = (counts + MOE_BLOCK - 1) // MOE_BLOCK * MOE_BLOCK
    pad_ends = jnp.cumsum(padded)
    pad_starts = pad_ends - padded
    dest = pad_starts[sorted_e] + jnp.arange(tk, dtype=jnp.int32) - starts[sorted_e]
    n_blocks = -(-tk // MOE_BLOCK) + N_EXPERTS
    n_rows = n_blocks * MOE_BLOCK
    row_tok = jnp.full((n_rows,), n_tok, jnp.int32).at[dest].set(order // TOP_K)
    row_w = jnp.zeros((n_rows,), flat_w.dtype).at[dest].set(flat_w[order])
    block_e = jnp.minimum(jnp.searchsorted(pad_ends, jnp.arange(n_blocks, dtype=jnp.int32) * MOE_BLOCK,
                                           side='right'), N_EXPERTS - 1)
    t_pad = jnp.concatenate([t, jnp.zeros((1, d), t.dtype)], axis=0)
    xs = t_pad[row_tok].reshape(n_blocks, MOE_BLOCK, d)

    def expert_block(args):
        xb, e = args
        hidden = jax.nn.silu(xb @ w1[e]) * (xb @ w3[e])
        return hidden @ w2[e]

    ys = lax.map(expert_block, (xs, block_e)).reshape(n_rows, d)
    out = jnp.zeros((n_tok + 1, d), ys.dtype).at[row_tok].add(ys * row_w[:, None].astype(ys.dtype))
    return out[:n_tok].reshape(b, l, d)

def setup_inputs(seed: int = 0) -> dict:
    key = jax.random.key(seed)
    ks = jax.random.split(key, 25)

    def nrm(k, shape, scale):
        return jax.random.normal(k, shape, jnp.float32) * scale

    def gain(k, shape):
        return 1.0 + nrm(k, shape, 0.02)

    dt0 = jnp.exp(jax.random.uniform(ks[11], (DEPTH, SSM_HEADS), jnp.float32,
                                     minval=math.log(1e-3), maxval=math.log(1e-1)))
    return {
        'x': nrm(ks[0], (BATCH, SEQ, D_MODEL), 1.0),
        'meta_tokens': nrm(ks[1], (N_META, D_MODEL), 1.0),
        'hg_lb_logits': 1.0 + nrm(ks[2], (DEPTH, HG_KEY), 0.1),
        'norm_mix_w': gain(ks[3], (DEPTH, D_MODEL)),
        'w_in': nrm(ks[4], (DEPTH, D_MODEL, D_IN), D_MODEL ** -0.5),
        'hg_norm_w': gain(ks[5], (DEPTH, HG_WIDTH)),
        'ml_b_i': nrm(ks[6], (DEPTH, ML_HEADS), 0.1),
        'ml_b_f': 3.0 + 3.0 * jax.random.uniform(ks[7], (DEPTH, ML_HEADS), jnp.float32),
        'ml_norm_w': gain(ks[8], (DEPTH, ML_WIDTH)),
        'ssm_conv_w': nrm(ks[9], (DEPTH, CONV_W, CONV_CH), CONV_W ** -0.5),
        'ssm_conv_b': nrm(ks[10], (DEPTH, CONV_CH), 0.01),
        'ssm_dt_bias': dt0 + jnp.log(-jnp.expm1(-dt0)),
        'ssm_a_log': jnp.log(jax.random.uniform(ks[12], (DEPTH, SSM_HEADS), jnp.float32, minval=1.0, maxval=16.0)),
        'ssm_d': 1.0 + nrm(ks[13], (DEPTH, SSM_HEADS), 0.1),
        'ssm_norm_w': gain(ks[14], (DEPTH, SSM_WIDTH)),
        'w_out': nrm(ks[15], (DEPTH, D_MIX, D_MODEL), D_MIX ** -0.5),
        'norm_ffn_w': gain(ks[16], (DEPTH, D_MODEL)),
        'moe_w_group': nrm(ks[17], (DEPTH, D_MODEL, N_GROUPS_MOE), D_MODEL ** -0.5),
        'moe_b_group': nrm(ks[18], (DEPTH, N_GROUPS_MOE), 0.01),
        'moe_w_router': nrm(ks[19], (DEPTH, N_GROUPS_MOE, D_MODEL, EXPERTS_PER_GROUP), D_MODEL ** -0.5),
        'moe_b_router': nrm(ks[20], (DEPTH, N_GROUPS_MOE, EXPERTS_PER_GROUP), 0.01),
        'moe_w1': nrm(ks[21], (DEPTH, N_EXPERTS, D_MODEL, D_EXPERT), D_MODEL ** -0.5),
        'moe_w3': nrm(ks[22], (DEPTH, N_EXPERTS, D_MODEL, D_EXPERT), D_MODEL ** -0.5),
        'moe_w2': nrm(ks[23], (DEPTH, N_EXPERTS, D_EXPERT, D_MODEL), D_EXPERT ** -0.5),
        'final_norm_w': gain(ks[24], (D_MODEL,)),
    }

def reference(x, meta_tokens, hg_lb_logits, norm_mix_w, w_in, hg_norm_w, ml_b_i, ml_b_f, ml_norm_w,
              ssm_conv_w, ssm_conv_b, ssm_dt_bias, ssm_a_log, ssm_d, ssm_norm_w, w_out, norm_ffn_w,
              moe_w_group, moe_b_group, moe_w_router, moe_b_router, moe_w1, moe_w3, moe_w2, final_norm_w):
    b = x.shape[0]
    meta = jnp.broadcast_to(meta_tokens.astype(x.dtype)[None], (b, N_META, D_MODEL))
    h = jnp.concatenate([meta, x], axis=1)
    lb_w = jax.nn.softmax(hg_lb_logits.astype(jnp.float32), axis=0)
    lower_bounds = jnp.cumsum(lb_w, axis=0) - lb_w[0]
    for layer in range(DEPTH):
        u = rmsnorm(h, norm_mix_w[layer])
        proj = (u @ w_in[layer]).astype(jnp.float32)
        (hq, hf, hi, hg, mq, mk, mv, mo, mi, mf, sz, sxbc, sdt) = split_last(proj, IN_SPLITS)
        y_a = hgrn2_mixer(hq, hf, hi, hg, lower_bounds[layer], hg_norm_w[layer])
        y_b = mlstm_mixer(mq, mk, mv, mo, mi, mf, ml_b_i[layer], ml_b_f[layer], ml_norm_w[layer])
        y_c = mamba2_mixer(sz, sxbc, sdt, ssm_conv_w[layer], ssm_conv_b[layer], ssm_dt_bias[layer],
                           ssm_a_log[layer], ssm_d[layer], ssm_norm_w[layer])
        mixed = jnp.concatenate([y_a, y_b, y_c], axis=-1).astype(h.dtype)
        h = h + mixed @ w_out[layer]
        h = h + hierarchical_moe(rmsnorm(h, norm_ffn_w[layer]), moe_w_group[layer], moe_b_group[layer],
                                 moe_w_router[layer], moe_b_router[layer], moe_w1[layer], moe_w3[layer],
                                 moe_w2[layer])
    return rmsnorm(h, final_norm_w)[:, N_META:]


_drawn_inputs = setup_inputs


def setup_inputs(seed=0):
    import zlib

    import numpy as np

    out = dict(_drawn_inputs(seed))
    spreads = {}
    factors = {'hg_norm_w': 21.475,
     'ml_b_i': 64.0,
     'ml_norm_w': 25.561,
     'ssm_conv_b': 4.201,
     'ssm_norm_w': 10.965,
     'moe_b_group': 23.173,
     'moe_b_router': 22.883,
     'final_norm_w': 8.087,
     'norm_ffn_w': 6.323}
    for name, (base, spread) in spreads.items():
        noise = np.random.default_rng([zlib.crc32(name.encode()), seed]).standard_normal(out[name].shape)
        drawn = base * np.exp(spread * noise) if base else spread * noise
        out[name] = jnp.asarray(drawn.astype(out[name].dtype))
    for name, factor in factors.items():
        out[name] = (out[name] * factor).astype(out[name].dtype)
    return out
```

```python
import numpy as np
import concourse.bass as bass
from concourse import mybir
from contextlib import ExitStack


class Steps:

    def __init__(self, eng, sem):
        self.eng, self.sem, self.n, self.reg, self.per = eng, sem, 0, None, 0

    def link(self, ins):
        ins.then_inc(self.sem, 1)
        self.n += 1
        self.eng.wait_ge(self.sem, self.n if self.reg is None else self.reg * self.per + self.n)

    def enter(self, reg, per):
        self.reg, self.per, self.before = reg, per, self.n

    def leave(self, passes):
        assert self.n - self.before == self.per, (self.n - self.before, self.per)
        self.n = self.before + self.per * passes
        self.reg = None


def hymba_moe_layer(nc, x, meta_tokens, hg_lb_logits, norm_mix_w, w_in, hg_norm_w, ml_b_i, ml_b_f,
                    ml_norm_w, ssm_conv_w, ssm_conv_b, ssm_dt_bias, ssm_a_log, ssm_d, ssm_norm_w,
                    w_out, norm_ffn_w, moe_w_group, moe_b_group, moe_w_router, moe_b_router,
                    moe_w1, moe_w3, moe_w2, final_norm_w, out):
    f32 = mybir.dt.float32
    i32 = mybir.dt.int32
    u32 = mybir.dt.uint32
    ALU = mybir.AluOpType
    ACT = mybir.ActivationFunctionType
    AX = mybir.AxisListType

    P = 128
    D = x.shape[2]
    NM = meta_tokens.shape[0]
    SEQ = x.shape[1]
    T = NM + SEQ
    KD = D // P
    TT = [(t, min(P, T - t)) for t in range(0, T, P)]
    NT = len(TT)
    TL = TT[-1][1]
    EPS = 1e-6
    HGH, MLH, SSH, SSG = 4, ml_b_i.shape[1], ssm_d.shape[1], 4
    MLQ = 64
    CONVW = ssm_conv_w.shape[1]
    GRP, EPG = moe_w_router.shape[1], moe_w_router.shape[3]
    NE = GRP * EPG
    FE = moe_w1.shape[3]
    KF = FE // P
    CAP = 64
    NB = -(-T // CAP)
    NOV = (2 * T) // (CAP + 1)
    NC_ = NB * NE

    C_IF = 3584
    C_Z = C_IF + 2 * MLH
    C_DT = C_Z + 3072
    CH = 256
    NG = 2 * MLH + SSH
    NFD = MLH + SSH

    Z0, X0, B0, C0 = 0, 8, 16, 20
    HQ, HF, HV, HG_, MQ, MK, MV, MO = 24, 28, 32, 36, 40, 42, 44, 48
    NP_ = 52
    MIXED = [HG_ + i for i in range(4)] + [MO + i for i in range(4)] + [Z0 + i for i in range(8)]

    PM, PF, PH_, PL, PS, PW, PB = 0, 16, 32, 36, 40, 48, 112

    SLOT = 4096
    NSLOT = 6
    WS0, WS1, WD = 272, 144, TL
    PW_ = WS0 + WS1 + WD

    ctx = ExitStack()
    with ctx:
        def sb(name, shape, dt=f32):
            return ctx.enter_context(nc.sbuf_tensor(name, shape, dt))

        def sem(name):
            return ctx.enter_context(nc.semaphore(name))

        ring = sb("ring", [P, NSLOT * SLOT])
        hT = sb("hT", [P, KD, T])
        uT = sb("uT", [P, KD, T])
        proj = sb("proj", [P, NP_, T])
        pflat = proj[:, :, :].rearrange("p a t -> p (a t)")

        def slot(j):
            return ring[:, j * SLOT:(j + 1) * SLOT]

        def wchunk(j):
            return slot(j).rearrange("p (k c) -> p k c", k=KD)

        xin = ring[:, 4 * SLOT:4 * SLOT + NT * D].rearrange("p (a d) -> p a d", a=NT)
        at = [2 * SLOT]

        def scr(n):
            at[0] += n
            assert at[0] <= NSLOT * SLOT
            return ring[:, at[0] - n:at[0]]

        sel = scr(NFD * P).rearrange("p (r c) -> p r c", r=NFD)
        EPb = scr(4 * PW_)
        E2 = EPb[:, 0:2 * PW_].rearrange("p (a c) -> p a c", a=2)
        P2 = EPb[:, 2 * PW_:4 * PW_].rearrange("p (a c) -> p a c", a=2)
        cumT = EPb[:, 0:4 * T].rearrange("p (h t) -> p h t", h=4)
        CBr = scr(4 * PW_)
        CB = CBr.rearrange("p (g c) -> p g c", g=4)
        rs4 = CBr[:, 0:4 * T].rearrange("p (h t) -> p h t", h=4)
        xv = scr(NT * 1024).rearrange("p (a c) -> p a c", a=NT)
        hv = scr(NT * 512).rearrange("p (a c) -> p a c", a=NT)
        mv = scr(NT * 512).rearrange("p (a c) -> p a c", a=NT)
        PHs = scr(4 * PW_).rearrange("p (h c) -> p h c", h=4)
        Wb = scr(2 * 4 * T)
        mden = Wb[:, 0:T]
        W = [Wb[:, i * 4 * T:(i + 1) * 4 * T].rearrange("p (h t) -> p h t", h=4) for i in range(2)]
        sq8 = Wb.rearrange("p (h t) -> p h t", h=8)
        conv = [Wb[:, i * T:(i + 1) * T] for i in range(4)]
        sqH = EPb[:, 0:4 * T].rearrange("p (h t) -> p h t", h=4)

        ident = sb("ident", [P, P])
        ones = sb("ones", [P, T])
        before = sb("before", [P, P])
        mcaus = sb("mcaus", [P, PW_])
        LV = [1, 2, 4, 8, 16, 32, 64]
        mlev = sb("mlev", [P, len(LV), P])
        par_rows = CBr[:, 0:P]
        lb_rows = CBr[:, P:2 * P]
        epsc = sb("epsc", [P, 1])
        fss = sb("fss", [P, 2])
        frs = sb("frs", [P, 2])
        par = sb("par", [P, P + 4])
        lb4 = sb("lb4", [P, 4, 4])
        wg = sb("wg", [P, KD, NG])
        wr = sb("wr", [P, KD, 36])
        brow = sb("brow", [P, 36])
        dB = sb("dB", [P, SSH])
        dcol = sb("dcol", [P, SSH // 2])
        gcols = sb("gcols", [NFD, 4])
        ss3 = sb("ss3", [P, NT])
        rs3 = sb("rs3", [P, NT])
        dg = EPb[:, 0:NT * P].rearrange("p (a c) -> p a c", a=NT)
        Rb = sb("Rb", [P, T])
        gX = sb("gX", [NFD, T])
        gA = hv[0:NFD, 0, 0:T]
        gZ = sb("gZ", [NFD, T])
        gQ = hv[0:NFD, 1, 0:T]
        gL = hv[0:MLH, 2, 0:T]
        gG = sb("gG", [MLH, T])
        colc = sb("colc", [P, NT, 2 * NFD + MLH])

        pb = [ctx.enter_context(nc.psum_tensor(f"bank{i}", [P, 512], f32)) for i in range(8)]

        moff = [0]

        def mo(n):
            moff[0] += n
            assert moff[0] <= NP_ * T
            return pflat[:, moff[0] - n:moff[0]]

        u2 = mo(NT * D).rearrange("p (a d) -> p a d", a=NT)
        h2 = pflat[:, 0:2 * D].rearrange("p (a d) -> p a d", a=2)
        xs = mo(1024)
        xsT = mo(1024).rearrange("p (c h s) -> p c h s", c=8, h=2)
        hs = mo(512)
        ssb = mo(KF * CAP).rearrange("p (k s) -> p k s", k=KF)
        hTb = mo(KF * CAP).rearrange("p (k s) -> p k s", k=KF)
        ysb = mo(1024)
        fw = uT[:, 0:8, :].rearrange("p k t -> p (k t)")[:, 0:D]
        hid_ps = pb[3][:, :].rearrange("p (k c) -> p k c", k=KF)
        rat = [moff[0]]

        def ro(n):
            rat[0] += n
            assert rat[0] <= NP_ * T
            return pflat[:, rat[0] - n:rat[0]]

        idx_base = sb("idx_base", [P, 3, NC_])
        idx_x = sb("idx_x", [P, NC_], i32)
        idx_y = sb("idx_y", [P, NC_], i32)
        ov_x = sb("ov_x", [P, NOV], i32)
        ov_y = sb("ov_y", [P, NOV], i32)
        ov_w = sb("ov_w", [P, NOV])
        ov_e = sb("ov_e", [P, NOV], i32)
        ov_n = sb("ov_n", [P, 1], i32)
        xcol = sb("xcol", [P, 1], i32)
        ycol = sb("ycol", [P, 1], i32)

        u2d = nc.dram_tensor("tokens_normed", (2 * T, 1024), f32, kind="Internal").ap()
        yd = nc.dram_tensor("expert_rows", (4 * T, 1024), f32, kind="Internal").ap()

        LH = LV + [P, 2 * P]
        NLEV = len(LH)
        LWID = [T if h <= 8 or h == 2 * P else 2 * P for h in LH]
        PAR_DMAS = 11

        s = {n: sem(n) for n in (
            "lg_ready iotas gmax pairs gmax_e ranks rhs_used rhs_ready idx_ready ov_ready x_in "
            "gatew_in in_a in_b in_ev h_ps y_ps y_out yt_in f_done out_sem pool_steps consts "
            "pool_waited xT_ps col_x xs_in col_y y_act y_dve ys_out y_free u2_out act_steps par_in "
            "routerw_in params_zeroed gate_cols_in rms_ready lb_diff lb_exp alog_exp x_T x_ev "
            "gi_ready gcols_ready li_ready fd_x fd_tanh fd_e em_t em_exp in_tile conv_acc "
            "conv_done xv_T xv_ev e_ready e_exp sq_ready sum_ready rs_ready ssm_gated hsig hlin "
            "hln hv_ev hv_T lv_d lv_e ml_e ml_exp ml_o ml_abs ml_h hg_done sq2 sum2 rs2 t_ps t_ev "
            "h2_ps h2_ev fw_in xT_ev h_ev hT_ps silu_ev f_sum f_rs dve_steps diag_ready par_T "
            "par_ev R_ready uT_ready gf_ready g_rows g_col g_colev cb_ready bc_ready y_ready "
            "pt_ready y_ev lv_ps lv_w lvd_ps lv_ev ho_ps ho_ev ml_ps ml_pt norm_done u2T_ready "
            "xT_ev2 hT_ready"
        ).split()}
        m_in = [sem(f"expert_in{j}") for j in range(NSLOT)]
        m_free = {j: sem(f"expert_free{j}") for j in (0, 1, 2, 4)}

        LG = GRP + NE
        io_e = ro(NE)
        io_s = ro(P)
        io_t = ro(2 * NT).rearrange("p (a j) -> p a j", j=2)
        io_c = ro(NC_ - NE)
        half = ro(1)
        L = ro(NT * LG).rearrange("p (a c) -> p a c", a=NT)
        rt_ex = ro(NT * 5).rearrange("p (a c) -> p a c", a=NT)
        g8, e8, mg, me_ = (ro(NT * 8).rearrange("p (a c) -> p a c", a=NT) for _ in range(4))
        ig, ie = (ro(NT * 8).bitcast(u32).rearrange("p (a c) -> p a c", a=NT) for _ in range(2))
        igf, gsum, wden = (ro(NT).rearrange("p (a c) -> p a c", a=NT) for _ in range(3))
        ief, w01, rankj, blk, slj, tj = (ro(NT * 2).rearrange("p (a c) -> p a c", a=NT) for _ in range(6))
        ohg = ro(NT * GRP).rearrange("p (a c) -> p a c", a=NT)
        esel = ro(NT * NE).rearrange("p (a g e) -> p a g e", a=NT, g=GRP)
        OH = ro(NT * 2 * NE).rearrange("p (a j e) -> p a j e", a=NT, j=2)
        rk2 = ro(NT * 2 * NE).rearrange("p (a j e) -> p a j e", a=NT, j=2)
        chosen = ro(NT * NE).rearrange("p (a e) -> p a e", a=NT)
        rankt = ro((NT + 1) * NE).rearrange("p (a e) -> p a e", e=NE)
        hot5 = ro(NT * 2 * NB).rearrange("p (a j b) -> p a j b", a=NT, j=2)
        slot_hot = [ro(P) for _ in range(2)]
        rhs_t = [ro(3 * NC_).rearrange("p (a c) -> p a c", a=3) for _ in range(2)]
        unused = ro(NC_)
        tmpc = ro(NC_)
        idxf = ro(2 * NC_).rearrange("p (a c) -> p a c", a=2)
        F_ = ro(NC_ - NE)
        O_ = ro(NC_ - NE)
        S_ = ro(NC_ - NE)
        Sj = ro(NC_ - NE)
        ovf = ro(4 * NOV).rearrange("p (a c) -> p a c", a=4)

        def routing(dve, V, step):
            def bc(ap, shape):
                return ap.to_broadcast(shape)

            V.memset(L, 0.0)
            V.memset(g8, -3e38)
            step.link(V.memset(rankt, 0.0))
            dve.wait_ge(s["lg_ready"], 1)
            for a, (_, n) in enumerate(TT):
                last = V.tensor_tensor(L[0:n, a, :], pb[5][0:n, a * LG:(a + 1) * LG], brow[0:n, :], ALU.add)
            step.link(last)
            step.link(V.tensor_copy(g8[:, :, 0:GRP], L[:, :, 0:GRP]))
            for a in range(NT):
                last = V.max(mg[:, a, :], g8[:, a, :])
            step.link(last)
            for a in range(NT):
                last = V.max_index(ig[:, a, :], mg[:, a, :], g8[:, a, :])
            step.link(last)
            step.link(V.tensor_copy(igf, ig[:, :, 0:1]))
            V.tensor_tensor(rt_ex[:, :, 0:GRP], L[:, :, 0:GRP], bc(mg[:, :, 0:1], [P, NT, GRP]), ALU.subtract)
            dve.wait_ge(s["iotas"], 1)
            step.link(V.tensor_tensor(ohg, io_e[:, 0:GRP].unsqueeze(1).to_broadcast([P, NT, GRP]),
                                      bc(igf, [P, NT, GRP]), ALU.is_equal))
            step.link(V.tensor_tensor(esel, L[:, :, GRP:LG].rearrange("p a (g e) -> p a g e", g=GRP),
                                      ohg.unsqueeze(3).to_broadcast([P, NT, GRP, EPG]), ALU.mult))
            step.link(V.tensor_reduce(e8, esel.rearrange("p a g e -> p a e g"), AX.X, ALU.add))
            for a in range(NT):
                last = V.max(me_[:, a, :], e8[:, a, :])
            step.link(last)
            for a in range(NT):
                V.max_index(ie[:, a, :], me_[:, a, :], e8[:, a, :])
            V.tensor_tensor(rt_ex[:, :, GRP:GRP + 1], me_[:, :, 1:2], me_[:, :, 0:1], ALU.subtract).then_inc(s["gmax"], 1)
            dve.wait_ge(s["gmax"], 1)
            step.link(V.tensor_copy(ief, ie[:, :, 0:2]))
            step.link(V.scalar_tensor_tensor(ief, bc(igf, [P, NT, 2]), float(EPG), ief, ALU.mult, ALU.add))
            for j in range(2):
                last = V.tensor_tensor(OH[:, :, j, :], io_e[:, 0:NE].unsqueeze(1).to_broadcast([P, NT, NE]),
                                       bc(ief[:, :, j:j + 1], [P, NT, NE]), ALU.is_equal)
            step.link(last)
            V.tensor_tensor(chosen, OH[:, :, 0, :], OH[:, :, 1, :], ALU.add).then_inc(s["pairs"], 1)
            dve.wait_ge(s["gmax_e"], 1)
            step.link(V.tensor_reduce(gsum, rt_ex[:, :, 0:GRP], AX.X, ALU.add))
            step.link(V.scalar_tensor_tensor(wden, rt_ex[:, :, GRP:GRP + 1], 1.0, gsum, ALU.add, ALU.mult))
            step.link(V.reciprocal(w01[:, :, 0:1], wden))
            V.tensor_tensor(w01[:, :, 1:2], w01[:, :, 0:1], rt_ex[:, :, GRP:GRP + 1], ALU.mult)
            dve.wait_ge(s["ranks"], 1)
            for a, (_, n) in enumerate(TT):
                V.tensor_copy(rankt[0:n, a, :], pb[6][0:n, a * NE:(a + 1) * NE])
            step.link(V.tensor_copy(rankt[:, NT, :], pb[6][:, NT * NE:(NT + 1) * NE]))
            for j in range(2):
                last = V.tensor_tensor(rk2[:, :, j, :], OH[:, :, j, :], rankt[:, 0:NT, :], ALU.mult)
            step.link(last)
            step.link(V.tensor_reduce(rankj, rk2, AX.X, ALU.add))
            step.link(V.tensor_scalar(blk, rankj, float(CAP), None, ALU.is_ge))
            for b in range(2, NB):
                step.link(V.scalar_tensor_tensor(blk, rankj, float(CAP * b), blk, ALU.is_ge, ALU.add))
            V.scalar_tensor_tensor(slj, blk, -float(CAP), rankj, ALU.mult, ALU.add)
            V.tensor_scalar(tj, io_t, 1.0, None, ALU.add)
            for j in range(2):
                last = V.tensor_tensor(hot5[:, :, j, :], io_e[:, 0:NB].unsqueeze(1).to_broadcast([P, NT, NB]),
                                       bc(blk[:, :, j:j + 1], [P, NT, NB]), ALU.is_equal)
            step.link(last)
            for m in range(2 * NT):
                a, j = m // 2, m % 2
                n = TT[a][1]
                if m >= 2:
                    dve.wait_ge(s["rhs_used"], m - 1)
                r = rhs_t[m % 2]
                V.tensor_scalar(slot_hot[m % 2][0:n, :], io_s[0:n, :], slj[0:n, a, j:j + 1], None, ALU.is_equal)
                step.link(V.tensor_tensor(r[0:n, 1, :].rearrange("p (b e) -> p b e", e=NE),
                                          OH[0:n, a, j, :].unsqueeze(1).to_broadcast([n, NB, NE]),
                                          hot5[0:n, a, j, :].unsqueeze(2).to_broadcast([n, NB, NE]), ALU.mult))
                V.tensor_scalar(r[0:n, 0, :], r[0:n, 1, :], tj[0:n, a, 0:1], None, ALU.mult)
                V.tensor_scalar(r[0:n, 2, :], r[0:n, 1, :], w01[0:n, a, j:j + 1], None, ALU.mult)
                V.tensor_scalar(r[0:n, 1, :], r[0:n, 1, :], tj[0:n, a, j:j + 1], None, ALU.mult).then_inc(
                    s["rhs_ready"], 1)
            dve.wait_ge(s["rhs_used"], 2 * NT)
            step.link(V.tensor_copy(idx_base[:, :, :].rearrange("p a c -> p (a c)"), pb[7][:, 0:3 * NC_]))
            step.link(V.tensor_scalar(unused, idx_base[:, 0, :], 0.5, 65536.0, ALU.is_lt, ALU.mult))
            step.link(V.tensor_scalar(unused, unused, half[:, 0:1], None, ALU.add))
            V.scalar_tensor_tensor(idxf[:, 0, :], idx_base[:, 0, :], -1.0, unused, ALU.add, ALU.add)
            step.link(V.scalar_tensor_tensor(tmpc, idx_base[:, 1, :], 2.0, unused, ALU.mult, ALU.add))
            step.link(V.tensor_scalar(idxf[:, 1, :], tmpc, -2.0, None, ALU.add))
            V.tensor_copy(idx_x[:, :], idxf[:, 0, :])
            V.tensor_copy(idx_y[:, :], idxf[:, 1, :]).then_inc(s["idx_ready"], 1)
            for b in range(1, NB):
                last = V.tensor_scalar(F_[:, (b - 1) * NE:b * NE], rankt[:, NT, :], float(CAP * b), None, ALU.is_gt)
            step.link(last)
            step.link(V.tensor_tensor_scan(O_, ones[:, 0:NC_ - NE], F_, 0.0, ALU.mult, ALU.add))
            step.link(V.tensor_copy(ov_n[:, :], O_[:, NC_ - NE - 1:NC_ - NE]))
            step.link(V.tensor_tensor(O_, O_, F_, ALU.subtract))
            for i in range(NOV):
                step.link(V.scalar_tensor_tensor(S_, O_, float(i), F_, ALU.is_equal, ALU.mult))
                for q, src in enumerate((idxf[:, 0, NE:NC_], idxf[:, 1, NE:NC_], idx_base[:, 2, NE:NC_], io_c)):
                    step.link(V.scalar_tensor_tensor(Sj, S_, 1.0, src, ALU.mult, ALU.mult,
                                                     accum_out=ovf[:, q, i:i + 1]))
            V.tensor_copy(ov_x[:, :], ovf[:, 0, :])
            V.tensor_copy(ov_y[:, :], ovf[:, 1, :])
            V.tensor_copy(ov_w[:, :], ovf[:, 2, :])
            V.tensor_copy(ov_e[:, :], ovf[:, 3, :]).then_inc(s["ov_ready"], 1)

        nc_block = ctx.enter_context(nc.Block())
        block = nc_block

        SC = [(0, 0, 0, T), (WS0, 1, P, T - P), (WS0 + WS1, 2, 2 * P, TL)]

        def columns(w, c):
            return w[0, :, bass.ds(c, CH)].rearrange("(k p) c -> p k c", p=P)

        @block.sync
        def _(sp):
            sp.dma_start(xin[0:NM, 0, :], meta_tokens[:, :]).then_inc(s["x_in"], 16)
            sp.dma_start(xin[NM:P, 0, :], x[0, 0:P - NM, :]).then_inc(s["x_in"], 16)
            sp.dma_start(xin[:, 1, :], x[0, P - NM:2 * P - NM, :]).then_inc(s["x_in"], 16)
            sp.dma_start(xin[0:TL, 2, :], x[0, 2 * P - NM:SEQ, :]).then_inc(s["x_in"], 16)
            sp.dma_start(wg[:, :, 0:2 * MLH],
                         w_in[0, :, C_IF:C_Z].rearrange("(k p) c -> p k c", p=P)).then_inc(s["gatew_in"], 16)
            sp.dma_start(wg[:, :, 2 * MLH:NG],
                         w_in[0, :, C_DT:C_DT + SSH].rearrange("(k p) c -> p k c", p=P)).then_inc(s["gatew_in"], 16)
            for w, first, passes, base in ((w_in, C_Z, 6, 0), (w_in, 0, 7, 6), (w_out, 0, 4, 13)):
                with sp.Fori(0, passes) as i:
                    for a, landed in enumerate((s["in_a"], s["in_b"])):
                        sp.wait_ge(s["in_ev"], i * 4 + (4 * base + 2 * a + 2))
                        sp.dma_start(wchunk(a), columns(w, i * (2 * CH) + (first + a * CH))).then_inc(landed, 16)

            def expert_weights(n, e):
                for j in range(NSLOT):
                    if j == 4:
                        sp.wait_ge(s["in_ev"], 4 * 17 + 4)
                    sp.wait_ge({3: s["h_ps"], 5: s["y_ps"]}[j] if j in (3, 5) else m_free[j], n + 1)
                    if j < 4:
                        w = (moe_w1, moe_w3)[j % 2]
                        src = w[0, bass.ds(e, 1), (j // 2) * 1024:(j // 2 + 1) * 1024, :].rearrange(
                            "e (k p) f -> p (e k) f", p=P)
                        dst = slot((j + 2) % 6).rearrange("p (k f) -> p k f", f=FE)
                    else:
                        src = moe_w2[0, bass.ds(e, 1), (j - 4) * 256:(j - 3) * 256, :].rearrange(
                            "e (k p) d -> p (e k) d", p=P)
                        dst = slot(j - 4).rearrange("p (k d) -> p k d", d=D)
                    sp.dma_start(dst, src).then_inc(m_in[j], 16)

            with sp.Fori(0, NE) as i:
                expert_weights(i, i)
            sp.wait_ge(s["ov_ready"], 1)
            count = sp.value_load(ov_n[0:1, 0:1], min_val=0, max_val=NOV)
            with sp.If(count > 0):
                with sp.Fori(0, count) as i:
                    e = sp.value_load(ov_e[0:1, bass.ds(i, 1)], min_val=0, max_val=NE - 1)
                    expert_weights(i + NE, e)
            for tb in range(2):
                if tb == 0:
                    sp.wait_ge(s["y_out"], 1)
                sp.dma_start(slot(tb).rearrange("p (j d) -> p j d", j=2),
                             yd[(NM + tb * P) * 4:(NM + (tb + 1) * P) * 4, :].rearrange(
                                 "(t j h) d -> t j (h d)", j=2, h=2)).then_inc(s["yt_in"], 16)
            for tb in range(2):
                sp.wait_ge(s["f_done"], tb + 1)
                sp.dma_start(out[0, tb * P:(tb + 1) * P, :], slot(tb)[:, 0:D]).then_inc(s["out_sem"], 16)
            sp.wait_ge(s["out_sem"], 32)

        @block.gpsimd
        def _(pool):
            V = nc.gpsimd
            step = Steps(pool, s["pool_steps"])
            V.memset(ones[:, :], 1.0)
            V.memset(ident[:, :], 0.0)
            V.memset(mcaus[:, :], 1.0)
            V.memset(mlev[:, :, :], 0.0)
            V.memset(before[:, :], 1.0)
            step.link(V.memset(sel[0:NFD, :, :], 0.0))
            V.affine_select(out=ident[:, :], in_=ident[:, :], compare_op=ALU.not_equal, fill=1.0, base=0,
                            pattern=[[-1, P]], channel_multiplier=1)
            V.affine_select(out=before[:, :], in_=before[:, :], compare_op=ALU.is_gt, fill=0.0, base=0,
                            pattern=[[1, P]], channel_multiplier=-1)
            for c, n in ((0, P), (WS0, P), (WS0 + WS1, TL)):
                V.affine_select(out=mcaus[:, c:c + n], in_=mcaus[:, c:c + n], compare_op=ALU.is_ge, fill=0.0,
                                base=0, pattern=[[1, n]], channel_multiplier=-1)
            V.affine_select(out=sel[0:NFD, :, :], in_=sel[0:NFD, :, :], compare_op=ALU.not_equal, fill=1.0,
                            base=0, pattern=[[-1, NFD], [0, P]], channel_multiplier=1)
            for li, h in enumerate(LV):
                m = mlev[:, li, :].rearrange("p (b r h) -> p b r h", r=2, h=h)[:, :, 1, :]
                step.link(V.memset(m, 1.0))
                step.link(V.affine_select(out=m, in_=m, compare_op=ALU.is_ge, fill=0.0, base=0,
                                          pattern=[[-2 * h, P // (2 * h)], [0, h]], channel_multiplier=1))
                last = V.affine_select(out=m, in_=m, compare_op=ALU.is_ge, fill=0.0, base=h - 1,
                                       pattern=[[2 * h, P // (2 * h)], [0, h]], channel_multiplier=-1)
            last.then_inc(s["consts"], 1)

            pool.wait_ge(s["in_ev"], 4 * 17 + 4)
            V.iota(io_e, pattern=[[1, NE]], base=0, channel_multiplier=0, allow_small_or_imprecise_dtypes=True)
            V.iota(io_s, pattern=[[0, 2], [1, CAP]], base=0, channel_multiplier=0,
                   allow_small_or_imprecise_dtypes=True)
            V.iota(io_t, pattern=[[2 * P, NT], [1, 2]], base=0, channel_multiplier=2,
                   allow_small_or_imprecise_dtypes=True)
            V.iota(io_c, pattern=[[0, NB - 1], [1, NE]], base=0, channel_multiplier=0,
                   allow_small_or_imprecise_dtypes=True)
            step.link(V.memset(half, 0.0))
            step.link(V.memset(half[64:P, :], 1.0))
            V.memset(xs, 0.0).then_inc(s["iotas"], 1)

            last_half, last_row = pool.to_reg(2 * T - 1), pool.to_reg(4 * T - 1)

            def waited():
                pool.sem_inc(s["pool_waited"], 1)

            def gather(m, col, freed=None):
                if freed is not None:
                    pool.wait_ge(s["xT_ps"], freed)
                    waited()
                V.tensor_copy(xcol[:, :], col).then_inc(s["col_x"], 1)
                pool.wait_ge(s["col_x"], m + 1)
                waited()
                V.indirect_dma_start(out=xs, out_offset=None, in_=u2d[:, :],
                                     in_offset=bass.IndirectOffsetOnAxis(ap=xcol[:, 0:1], axis=0),
                                     bounds_check=last_half, oob_is_err=False).then_inc(s["xs_in"], 16)

            def scatter(n, col):
                V.tensor_copy(ycol[:, :], col).then_inc(s["col_y"], 1)
                pool.wait_ge(s["col_y"], n + 1)
                pool.wait_ge(s["y_act"], n + 1)
                pool.wait_ge(s["y_dve"], n + 1)
                waited()
                V.indirect_dma_start(out=yd[:, :],
                                     out_offset=bass.IndirectOffsetOnAxis(ap=ycol[:, 0:1], axis=0),
                                     in_=ysb, in_offset=None,
                                     bounds_check=last_row, oob_is_err=False).then_inc(s["ys_out"], 16)
                pool.wait_ge(s["ys_out"], n * 16 + 16)
                pool.sem_inc(s["y_free"], 1)

            pool.wait_ge(s["u2_out"], NT * 16)
            pool.wait_ge(s["idx_ready"], 1)
            pool.sem_inc(s["y_free"], 1)
            gather(0, idx_x[:, 0:1])
            with pool.Fori(0, NE) as i:
                gather(i + 1, idx_x[:, bass.ds(i + 1, 1)], i + 1)
                scatter(i, idx_y[:, bass.ds(i, 1)])
            pool.wait_ge(s["xs_in"], NE * 16 + 16)
            pool.wait_ge(s["ov_ready"], 1)
            count = pool.value_load(ov_n[0:1, 0:1], min_val=0, max_val=NOV)
            with pool.If(count > 0):
                with pool.Fori(0, count) as i:
                    gather(i + (NE + 1), ov_x[:, bass.ds(i, 1)], i + NE)
                    scatter(i + NE, ov_y[:, bass.ds(i, 1)])
            V.memset(xcol[:, :], 0).then_inc(s["y_out"], 1)

        @block.scalar
        def _(act):
            V = nc.scalar
            step = Steps(act, s["act_steps"])
            par_dmas = [(par_rows[PM:PM + 16, :], norm_mix_w[0].rearrange("(r c) -> r c", c=P)),
                        (par_rows[PF:PF + 16, :], norm_ffn_w[0].rearrange("(r c) -> r c", c=P)),
                        (par_rows[PH_:PH_ + 4, :], hg_norm_w[0].rearrange("(r c) -> r c", c=P)),
                        (par_rows[PL:PL + 4, :], ml_norm_w[0].rearrange("(r c) -> r c", c=P)),
                        (par_rows[PS:PS + 8, :], ssm_norm_w[0].rearrange("(r c) -> r c", c=P)),
                        (par_rows[PW:PW + 64, :], ssm_conv_w[0].rearrange("j (r c) -> (j r) c", c=P)),
                        (par_rows[PB:PB + 16, :], ssm_conv_b[0].rearrange("(r c) -> r c", c=P)),
                        (lb_rows[0:4, :], hg_lb_logits[0].rearrange("(r c) -> r c", c=P)),
                        (dB[:, :], ssm_d[0].partition_broadcast(P)),
                        (brow[:, 0:GRP], moe_b_group[0].partition_broadcast(P)),
                        (brow[:, GRP:GRP + NE], moe_b_router[0].rearrange("g e -> (g e)").partition_broadcast(P))]
            for dst, src in par_dmas:
                act.dma_start(dst, src).then_inc(s["par_in"], 16)
            assert len(par_dmas) == PAR_DMAS
            act.dma_start(wr[:, :, 0:GRP], moe_w_group[0].rearrange("(k p) g -> p k g", p=P)).then_inc(s["routerw_in"], 16)
            for g in range(GRP):
                act.dma_start(wr[:, :, GRP + g * EPG:GRP + (g + 1) * EPG],
                              moe_w_router[0, g].rearrange("(k p) e -> p k e", p=P)).then_inc(s["routerw_in"], 16)
            act.wait_ge(s["params_zeroed"], 1)
            for dst, src in ((gcols[0:MLH, 0:1], ml_b_f), (gcols[MLH:NFD, 0:1], ssm_dt_bias),
                             (gcols[MLH:NFD, 1:2], ssm_a_log), (gcols[0:MLH, 2:3], ml_b_i)):
                act.dma_start(dst, src[0].rearrange("(r c) -> r c", c=1)).then_inc(s["gate_cols_in"], 16)

            act.wait_ge(s["x_in"], 64)
            junk = uT[:, 0:8, :].rearrange("p k t -> p (k t)")[:, 0:D]
            for a, (_, n) in enumerate(TT):
                if a:
                    act.wait_ge(s["act_steps"], step.n)
                step.link(V.activation(junk[0:n, :], xin[0:n, a, :], ACT.Square, accum_out=ss3[0:n, a:a + 1]))
            step.link(V.activation(rs3[:, :], ss3[:, :], ACT.Ln, scale=1.0 / D, bias=epsc[:, 0:1]))
            V.activation(rs3[:, :], rs3[:, :], ACT.Exp, scale=-0.5).then_inc(s["rms_ready"], 1)
            act.wait_ge(s["lb_diff"], 1)
            V.activation(lb4[:, 1, :], lb4[:, 0, :], ACT.Exp).then_inc(s["lb_exp"], 1)
            act.wait_ge(s["gate_cols_in"], 64)
            V.activation(gcols[:, 1:2], gcols[:, 1:2], ACT.Exp).then_inc(s["alog_exp"], 1)
            for k in range(KD):
                act.wait_ge(s["x_T"], k + 1)
                V.activation(hT[:, k, :], pb[k % 4][:, 0:T], ACT.Copy).then_inc(s["x_ev"], 1)

            act.wait_ge(s["gi_ready"], 1)
            act.wait_ge(s["gcols_ready"], 1)
            V.activation(gL[:, :], pb[4][0:MLH, 0:T], ACT.Tanh, scale=1.0 / 15, bias=gcols[0:MLH, 2:3]).then_inc(
                s["li_ready"], 1)
            act.wait_ge(s["fd_x"], 1)
            V.activation(gX[0:MLH, :], gX[0:MLH, :], ACT.Tanh, scale=1.0 / 15).then_inc(s["fd_tanh"], 1)
            act.wait_ge(s["fd_x"], 2)
            step.link(V.activation(gQ[:, :], gX[:, :], ACT.Abs))
            V.activation(gQ[:, :], gQ[:, :], ACT.Exp, scale=-1.0).then_inc(s["fd_e"], 1)
            act.wait_ge(s["em_t"], 1)
            V.activation(gZ[0:MLH, :], gZ[0:MLH, :], ACT.Exp, scale=-1.0).then_inc(s["em_exp"], 1)

            def tiles_out(i, base, func):
                for b in range(4):
                    act.wait_ge(s["in_tile"], i * 4 + (4 * base + b + 1))
                    V.activation(proj[:, bass.ds(i * 4 + (4 * base + b), 1), :].rearrange("p a t -> p (a t)"),
                                 pb[b][:, 0:T], func).then_inc(s["in_ev"], 1)

            def conv_out(i, b):
                act.wait_ge(s["conv_acc"], i * 4 + (b + 1))
                V.activation(proj[:, bass.ds(i * 4 + (X0 + b), 1), :].rearrange("p a t -> p (a t)"),
                             conv[b], ACT.Silu).then_inc(s["conv_done"], 1)

            act.sem_inc(s["in_ev"], 4)
            act.sem_inc(s["conv_done"], 4)
            with act.Fori(0, 2) as i:
                tiles_out(i, 0, ACT.Silu)
            with act.Fori(0, 4) as i:
                tiles_out(i, 2, ACT.Copy)
            with act.Fori(0, 3) as i:
                tiles_out(i, 6, ACT.Copy)
                for b in range(4):
                    conv_out(i, b)
            tiles_out(0, 9, ACT.Silu)
            for b in range(4):
                conv_out(3, b)

            for a, (_, n) in enumerate(TT):
                for hf_ in range(2):
                    act.wait_ge(s["xv_T"], 2 * a + hf_ + 1)
                    V.activation(xv[0:n, a, hf_ * 512:(hf_ + 1) * 512], pb[(2 * a + hf_) % 4][0:n, :],
                                 ACT.Copy).then_inc(s["xv_ev"], 1)

            for e in range(SSH):
                act.wait_ge(s["e_ready"], e + 1)
                V.activation(E2[:, e % 2, 0:WS0 + WS1], E2[:, e % 2, 0:WS0 + WS1], ACT.Exp)
                V.activation(E2[0:TL, e % 2, WS0 + WS1:PW_], E2[0:TL, e % 2, WS0 + WS1:PW_], ACT.Exp).then_inc(
                    s["e_exp"], 1)

            norm_no = [0]

            def group_norm(made, count, src, sq, groups, tiles, banks):
                width = groups * tiles
                act.wait_ge(made, count)
                V.activation(sq[:, 0:width, :], src, ACT.Square).then_inc(s["sq_ready"], 1)
                for g in range(groups):
                    act.wait_ge(s["sum_ready"], 4 * norm_no[0] + g + 1)
                    last = V.activation(rs4[:, g, :], pb[banks + g][:, 0:T], ACT.Ln, scale=1.0 / (P * tiles),
                                        bias=epsc[:, 0:1])
                step.link(last)
                V.activation(rs4[:, :, :], rs4[:, :, :], ACT.Exp, scale=-0.5).then_inc(s["rs_ready"], 1)
                norm_no[0] += 1

            group_norm(s["ssm_gated"], 1, proj[:, Z0:Z0 + 8, :], sq8, 4, 2, 4)

            with act.Fori(0, 2) as i:
                tiles_out(i, 10, ACT.Copy)
            tiles_out(0, 12, ACT.Sigmoid)

            act.wait_ge(s["in_ev"], HF + 4 + 4)
            V.activation(W[0][:, :, :], proj[:, HF:HF + 4, :], ACT.Sigmoid).then_inc(s["hsig"], 1)
            V.activation(proj[:, HF:HF + 4, :], proj[:, HF:HF + 4, :], ACT.Sigmoid, scale=-1.0).then_inc(s["hsig"], 1)
            act.wait_ge(s["hlin"], 1)
            V.activation(W[0][:, :, :], W[0][:, :, :], ACT.Ln).then_inc(s["hln"], 1)
            for m, (dst, done) in enumerate(((hv, s["hv_ev"]), (mv, s["hv_ev"]))):
                for a, (_, n) in enumerate(TT):
                    act.wait_ge(s["hv_T"], 3 * m + a + 1)
                    V.activation(dst[0:n, a, :], pb[6 + (3 * m + a) % 2][0:n, :], ACT.Copy).then_inc(done, 1)
            for l in range(NLEV):
                act.wait_ge(s["lv_d"], l + 1)
                n = LWID[l]
                V.activation(W[l % 2][:, :, 0:n], W[l % 2][:, :, 0:n], ACT.Exp).then_inc(s["lv_e"], 1)
            for h in range(MLH):
                act.wait_ge(s["ml_e"], h + 1)
                V.activation(E2[:, h % 2, 0:WS0 + WS1], E2[:, h % 2, 0:WS0 + WS1], ACT.Exp, scale=-1.0)
                V.activation(E2[0:TL, h % 2, WS0 + WS1:PW_], E2[0:TL, h % 2, WS0 + WS1:PW_], ACT.Exp,
                             scale=-1.0).then_inc(s["ml_exp"], 1)
                act.wait_ge(s["ml_o"], h + 1)
                V.activation(mden[:, :], pb[3][:, 0:T], ACT.Abs).then_inc(s["ml_abs"], 1)
            group_norm(s["ml_h"], MLH, proj[:, HQ:HQ + 4, :], sqH, 4, 1, 4)
            group_norm(s["hg_done"], 1, W[1][:, :, :], sqH, 4, 1, 4)

            for k in range(KD):
                act.wait_ge(s["in_ev"], 4 * 13 + 4 + k + 1)
                V.activation(uT[:, k, :], hT[:, k, :], ACT.Square).then_inc(s["sq2"], 1)
            act.wait_ge(s["sum2"], 1)
            step.link(V.activation(Rb[:, :], pb[4][:, 0:T], ACT.Ln, scale=1.0 / D, bias=epsc[:, 0:1]))
            V.activation(Rb[:, :], Rb[:, :], ACT.Exp, scale=-0.5).then_inc(s["rs2"], 1)
            for a, (_, n) in enumerate(TT):
                for q in range(4):
                    act.wait_ge(s["t_ps"], 4 * a + q + 1)
                    V.activation(u2[0:n, a, q * 512:(q + 1) * 512], pb[q][0:n, :], ACT.Copy).then_inc(s["t_ev"], 1)
                act.wait_ge(s["t_ev"], 4 * a + 4)
                t0 = TT[a][0]
                act.dma_start(u2d[2 * t0:2 * (t0 + n), :].rearrange("(t h) d -> t (h d)", h=2),
                              u2[0:n, a, :]).then_inc(s["u2_out"], 16)
            act.wait_ge(s["gmax"], 1)
            V.activation(rt_ex, rt_ex, ACT.Exp).then_inc(s["gmax_e"], 1)
            act.wait_ge(s["u2_out"], NT * 16)
            for tb in range(2):
                for q in range(4):
                    act.wait_ge(s["h2_ps"], 4 * tb + q + 1)
                    V.activation(h2[:, tb, q * 512:(q + 1) * 512], pb[4 * tb + q][:, :], ACT.Copy).then_inc(
                        s["h2_ev"], 1)
            act.dma_start(fw, final_norm_w.partition_broadcast(P)).then_inc(s["fw_in"], 16)

            def expert(n, wcol):
                act.wait_ge(s["xT_ps"], n + 1)
                V.activation(xsT[:, 0:4, :, :].rearrange("p c h s -> p (c h s)"), pb[0][:, :],
                             ACT.Copy).then_inc(s["xT_ev"], 1)
                act.wait_ge(s["h_ps"], n + 2)
                V.activation(hs, pb[2][:, :], ACT.Copy).then_inc(s["h_ev"], 1)
                act.wait_ge(s["hT_ps"], n + 1)
                V.activation(ssb, hid_ps[:, :, 0:CAP], ACT.Silu).then_inc(s["silu_ev"], 1)
                act.wait_ge(s["y_ps"], n + 2)
                act.wait_ge(s["y_free"], n + 1)
                V.activation(ysb[:, 0:512], pb[4][:, :], ACT.Copy, scale=wcol).then_inc(s["y_act"], 1)

            with act.Fori(0, NE) as i:
                expert(i, idx_base[:, 2, bass.ds(i, 1)])
            act.wait_ge(s["ov_ready"], 1)
            count = act.value_load(ov_n[0:1, 0:1], min_val=0, max_val=NOV)
            with act.If(count > 0):
                with act.Fori(0, count) as i:
                    expert(i + NE, ov_w[:, bass.ds(i, 1)])
            for tb in range(2):
                act.wait_ge(s["f_sum"], tb + 1)
                step.link(V.activation(slot(tb)[:, D:2 * D], h2[:, tb, :], ACT.Square,
                                       accum_out=fss[:, tb:tb + 1]))
                step.link(V.activation(frs[:, tb:tb + 1], fss[:, tb:tb + 1], ACT.Ln, scale=1.0 / D,
                                       bias=epsc[:, 0:1]))
                V.activation(frs[:, tb:tb + 1], frs[:, tb:tb + 1], ACT.Exp, scale=-0.5).then_inc(s["f_rs"], 1)

        @block.vector
        def _(dve):
            V = nc.vector
            step = Steps(dve, s["dve_steps"])
            V.memset(epsc[:, :], EPS)
            V.memset(ss3[:, :], 1.0)
            V.memset(gcols[:, :], 0.0).then_inc(s["params_zeroed"], 1)
            dve.wait_ge(s["consts"], 1)
            dve.wait_ge(s["rms_ready"], 1)
            for a, (_, n) in enumerate(TT):
                last = V.tensor_scalar(dg[0:n, a, 0:n], ident[0:n, 0:n], rs3[0:n, a:a + 1], None, ALU.mult)
            last.then_inc(s["diag_ready"], 1)
            dve.wait_ge(s["par_T"], 1)
            V.tensor_copy(par[:, :], pb[7][:, 0:P + 4]).then_inc(s["par_ev"], 1)
            dve.wait_ge(s["par_ev"], 1)
            V.tensor_tensor(lb4[:, 0, :], par[:, P:P + 4], par[:, P:P + 4], ALU.subtract).then_inc(s["lb_diff"], 1)
            dve.wait_ge(s["lb_exp"], 1)
            step.link(V.reciprocal(lb4[:, 2, :], lb4[:, 1, :]))
            step.link(V.tensor_tensor(lb4[:, 0, :], lb4[:, 1, :], lb4[:, 2, :], ALU.mult))
            step.link(V.tensor_tensor(lb4[:, 3, :], lb4[:, 0, :], lb4[:, 0, :], ALU.subtract))
            step.link(V.tensor_scalar(lb4[:, 1, :], lb4[:, 3, :], 1e-30, None, ALU.max))
            V.tensor_scalar(lb4[:, 0, :], lb4[:, 3, :], -1.0, 1.0, ALU.mult, ALU.add)
            step.link(V.tensor_tensor(lb4[:, 2, :], lb4[:, 3, :], lb4[:, 1, :], ALU.subtract))
            V.tensor_copy(dcol[0:64, :], dB[0:64, :].rearrange("p (c r) -> p c r", r=2)[:, :, 0])
            step.link(V.tensor_copy(dcol[64:P, :], dB[64:P, :].rearrange("p (c r) -> p c r", r=2)[:, :, 1]))
            dve.wait_ge(s["alog_exp"], 1)
            V.tensor_scalar(gcols[:, 1:2], gcols[:, 1:2], -1.0, None, ALU.mult)
            V.tensor_scalar(gcols[:, 2:3], gcols[:, 2:3], 1.0 / 15, None, ALU.mult).then_inc(s["gcols_ready"], 1)
            dve.wait_ge(s["R_ready"], 1)
            step.link(V.tensor_copy(Rb[:, :], pb[6][:, 0:T]))
            for k in range(KD):
                dve.wait_ge(s["x_ev"], k + 1)
                V.scalar_tensor_tensor(uT[:, k, :], hT[:, k, :], par[:, PM + k:PM + k + 1], Rb[:, :],
                                       ALU.mult, ALU.mult).then_inc(s["uT_ready"], 1)

            dve.wait_ge(s["gf_ready"], 1)
            dve.wait_ge(s["gcols_ready"], 1)
            V.tensor_scalar(gX[:, :], pb[5][0:NFD, 0:T], gcols[:, 0:1], None, ALU.add).then_inc(s["fd_x"], 1)
            dve.wait_ge(s["fd_tanh"], 1)
            V.tensor_scalar(gX[0:MLH, :], gX[0:MLH, :], -15.0, None, ALU.mult).then_inc(s["fd_x"], 1)
            dve.wait_ge(s["fd_e"], 1)
            step.link(V.tensor_scalar(gA[:, :], gQ[:, :], 2.0, None, ALU.add))
            step.link(V.reciprocal(gZ[:, :], gA[:, :]))
            step.link(V.tensor_tensor(gA[:, :], gQ[:, :], gZ[:, :], ALU.mult))
            step.link(V.tensor_tensor(gZ[:, :], gA[:, :], gA[:, :], ALU.mult))
            step.link(V.tensor_scalar(gQ[:, :], gZ[:, :], 1.0 / 15, None, ALU.mult))
            for c in (13, 11, 9, 7, 5, 3):
                step.link(V.scalar_tensor_tensor(gQ[:, :], gQ[:, :], 1.0 / c, gZ[:, :], ALU.add, ALU.mult))
            step.link(V.scalar_tensor_tensor(gQ[:, :], gQ[:, :], 1.0, gA[:, :], ALU.add, ALU.mult))
            step.link(V.tensor_scalar(gX[:, :], gX[:, :], 0.0, None, ALU.max))
            step.link(V.scalar_tensor_tensor(gA[:, :], gQ[:, :], 2.0, gX[:, :], ALU.mult, ALU.add))
            step.link(V.tensor_scalar(gQ[:, :], gA[:, :], gcols[:, 1:2], None, ALU.mult))
            step.link(V.tensor_tensor_scan(gX[:, :], ones[0:NFD, :], gQ[:, :], 0.0, ALU.mult, ALU.add))
            dve.wait_ge(s["li_ready"], 1)
            step.link(V.scalar_tensor_tensor(gL[:, :], gL[:, :], 15.0, gX[0:MLH, :], ALU.mult, ALU.subtract))
            step.link(V.tensor_tensor_scan(gG[:, :], gL[:, :], gL[:, :], 0.0, ALU.max, ALU.max))
            V.tensor_tensor(gZ[0:MLH, :], gG[:, :], gX[0:MLH, :], ALU.add).then_inc(s["em_t"], 1)
            dve.wait_ge(s["em_exp"], 1)
            V.tensor_scalar(gZ[0:MLH, :], gZ[0:MLH, :], 1e37, None, ALU.min).then_inc(s["g_rows"], 1)
            dve.wait_ge(s["g_col"], 1)
            for a, (_, n) in enumerate(TT):
                last = V.tensor_copy(colc[0:n, a, :], pb[6][0:n, 64 * a:64 * a + 2 * NFD + MLH])
            last.then_inc(s["g_colev"], 1)
            dve.wait_ge(s["g_colev"], 1)

            with dve.Fori(0, 4) as i:
                step.enter(i, 12)
                for b in range(4):
                    dve.wait_ge(s["in_ev"], i * 4 + (X0 + b + 1 + 4))
                    dve.wait_ge(s["conv_done"], i * 4 + (b + 1))
                    raw = proj[:, bass.ds(i * 4 + (X0 + b), 1), :].rearrange("p a t -> p (a t)")

                    def tap(j):
                        return par[:, bass.ds(i * 4 + (PW + 16 * j + b), 1)]

                    step.link(V.tensor_scalar(conv[b], raw, tap(3), par[:, bass.ds(i * 4 + (PB + b), 1)],
                                              ALU.mult, ALU.add))
                    for j in (2, 1, 0):
                        d = CONVW - 1 - j
                        shifted = proj[:, bass.ds(i * 4 + (X0 + b), 1), 0:T - d].rearrange("p a t -> p (a t)")
                        last = V.scalar_tensor_tensor(conv[b][:, d:T], shifted, tap(j), conv[b][:, d:T],
                                                      ALU.mult, ALU.add)
                        if j:
                            step.link(last)
                    last.then_inc(s["conv_acc"], 1)
                step.leave(4)

            for g in range(SSG):
                dve.wait_ge(s["cb_ready"], g + 1)
                V.tensor_tensor(CB[:, g, 0:WS0 + WS1], pb[4 + g][:, 0:WS0 + WS1], mcaus[:, 0:WS0 + WS1], ALU.mult)
                last = V.tensor_tensor(CB[0:TL, g, WS0 + WS1:PW_], pb[4 + g][0:TL, WS0 + WS1:PW_],
                                       mcaus[0:TL, WS0 + WS1:PW_], ALU.mult)
            step.link(last)
            last = None

            def ssm_decay(e):
                dve.wait_ge(s["bc_ready"], e + 1)
                for c, a, t, n in SC:
                    r = TT[a][1]
                    last = V.tensor_scalar(E2[0:r, e % 2, c:c + n], pb[e % 2][0:r, t:t + n],
                                           colc[0:r, a, MLH + e:MLH + e + 1], 0.0, ALU.subtract, ALU.min)
                last.then_inc(s["e_ready"], 1)

            def ssm_scores(e):
                dve.wait_ge(s["e_exp"], e + 1)
                if e >= 2:
                    dve.wait_ge(s["y_ready"], e - 1)
                for c, a, t, n in SC:
                    r = TT[a][1]
                    last = V.scalar_tensor_tensor(P2[0:r, e % 2, c:c + n], E2[0:r, e % 2, c:c + n],
                                                  colc[0:r, a, NFD + MLH + e:NFD + MLH + e + 1],
                                                  CB[0:r, e // 4, c:c + n], ALU.mult, ALU.mult)
                last.then_inc(s["pt_ready"], 1)

            def ssm_out(c):
                dve.wait_ge(s["y_ready"], 2 * c + 2)
                V.scalar_tensor_tensor(proj[:, X0 + c, :], proj[:, X0 + c, :], dcol[:, c:c + 1],
                                       pb[2 + c % 2][:, 0:T], ALU.mult, ALU.add).then_inc(s["y_ev"], 1)
                dve.wait_ge(s["y_ev"], c + 1)
                return V.tensor_tensor(proj[:, Z0 + c, :], proj[:, Z0 + c, :], proj[:, X0 + c, :], ALU.mult)

            for e in range(SSH + 1):
                if e < SSH:
                    ssm_decay(e)
                if e >= 1:
                    ssm_scores(e - 1)
                if e >= 4 and e % 2 == 0:
                    ssm_out(e // 2 - 2)
            ssm_out(SSH // 2 - 1).then_inc(s["ssm_gated"], 1)
            norm_no = [0]

            def group_norm(src, dst, gate, groups, tiles, pcol):
                dve.wait_ge(s["rs_ready"], norm_no[0] + 1)
                for c in range(groups * tiles):
                    last = V.scalar_tensor_tensor(dst(c), src(c), par[:, pcol + c:pcol + c + 1],
                                                  rs4[:, c // tiles, :], ALU.mult, ALU.mult)
                if gate is not None:
                    step.link(last)
                    for c in range(groups * tiles):
                        last = V.tensor_tensor(gate(c), gate(c), dst(c), ALU.mult)
                norm_no[0] += 1
                return last

            group_norm(lambda c: proj[:, Z0 + c, :], lambda c: proj[:, Z0 + c, :], None, 4, 2, PS)

            dve.wait_ge(s["hsig"], 2)
            for h in range(HGH):
                V.tensor_scalar(W[0][:, h, :], W[0][:, h, :], lb4[:, 0, h:h + 1], lb4[:, 1, h:h + 1],
                                ALU.mult, ALU.add)
                V.tensor_scalar(proj[:, HF + h, :], proj[:, HF + h, :], lb4[:, 0, h:h + 1],
                                lb4[:, 2, h:h + 1], ALU.mult, ALU.add)
            V.tensor_scalar(proj[:, HQ:HQ + 4, :], proj[:, HQ:HQ + 4, :], float(P) ** -0.5, None,
                            ALU.mult).then_inc(s["hlin"], 1)
            V.memset(PHs[:, :, :], 0.0)
            dve.wait_ge(s["hln"], 1)
            for h in range(HGH):
                last = V.tensor_tensor_scan(cumT[:, h, :], ones[:, :], W[0][:, h, :], 0.0, ALU.mult, ALU.add)
            step.link(last)

            def halves(t, l):
                h = LH[l]
                if l == NLEV - 1:
                    return t[:, :, 0:2 * P], t[:, :, 2 * P:T]
                if h <= 8:
                    v = t.rearrange("p a (b r h) -> p (a b) r h", r=2, h=h)
                    return v[:, :, 0, :], v[:, :, 1, :]
                v = t[:, :, 0:2 * P].rearrange("p a (b r h) -> p a b r h", r=2, h=h)
                return v[:, :, :, 0, :], v[:, :, :, 1, :]

            def level_diff(l):
                if l >= 2:
                    dve.wait_ge(s["lv_ps"], l - 1)
                h = LH[l]
                cl, cr = halves(cumT, l)
                wl, wr_ = halves(W[l % 2], l)
                ref = cl[:, :, h - 1:h] if len(cl.shape) == 3 else cl[:, :, :, h - 1:h]
                V.tensor_tensor(wl, ref.to_broadcast(list(cl.shape)), cl, ALU.subtract)
                V.tensor_tensor(wr_, cr, ref.to_broadcast(list(cr.shape)), ALU.subtract).then_inc(s["lv_d"], 1)

            def level_scale(l):
                dve.wait_ge(s["lv_e"], l + 1)
                wl, wr_ = halves(W[l % 2], l)
                kl, _ = halves(proj[:, HF:HF + 4, :], l)
                _, qr = halves(proj[:, HQ:HQ + 4, :], l)
                V.tensor_tensor(wl, wl, kl, ALU.mult)
                V.tensor_tensor(wr_, wr_, qr, ALU.mult).then_inc(s["lv_w"], 1)

            def level_store(l):
                if l < 0:
                    dve.wait_ge(s["lvd_ps"], 1)
                else:
                    dve.wait_ge(s["lv_ps"], l + 1)
                    dve.wait_ge(s["lv_ev"], l + 1)
                b = 3 * ((l + 1) % 2)
                if l < 7:
                    m = ident[:, :] if l < 0 else mlev[:, l, :]
                    m = m.bitcast(u32)
                    for a in range(2):
                        c = (0, WS0)[a]
                        last = V.copy_predicated(
                            PHs[:, :, c:c + P], m.unsqueeze(1).to_broadcast([P, 4, P]),
                            pb[b + a][:, :].rearrange("p (h t) -> p h t", h=4))
                    if l < 0 or LH[l] <= 8:
                        last = V.copy_predicated(
                            PHs[0:TL, :, WS0 + WS1:PW_], m[0:TL, 0:TL].unsqueeze(1).to_broadcast([TL, 4, TL]),
                            pb[b + 2][0:TL, 0:4 * TL].rearrange("p (h t) -> p h t", h=4))
                elif l == 7:
                    last = V.tensor_copy(PHs[:, :, P:2 * P], pb[b][:, :].rearrange("p (h t) -> p h t", h=4))
                else:
                    v = pb[b][:, 0:8 * TL].rearrange("p (a h t) -> p a h t", a=2, h=4)
                    V.tensor_copy(PHs[:, :, 2 * P:T], v[:, 0, :, :])
                    last = V.tensor_copy(PHs[:, :, T + P:T + WS1], v[:, 1, :, :])
                last.then_inc(s["lv_ev"], 1)

            level_diff(0)
            level_store(-1)
            for l in range(NLEV):
                if l + 1 < NLEV:
                    level_diff(l + 1)
                level_scale(l)
                if l >= 1:
                    level_store(l - 1)
            level_store(NLEV - 1)
            for h in range(HGH):
                dve.wait_ge(s["ho_ps"], h + 1)
                last = V.tensor_copy(proj[:, HQ + h, :], pb[4 + h % 2][:, 0:T])
                last.then_inc(s["ho_ev"], 1)

            for h in range(MLH):
                dve.wait_ge(s["ml_ps"], h + 1)
                for c, a, t, n in SC:
                    r = TT[a][1]
                    last = V.tensor_scalar(E2[0:r, h % 2, c:c + n], pb[1][0:r, t:t + n],
                                           colc[0:r, a, 2 * NFD + h:2 * NFD + h + 1], 0.0, ALU.subtract, ALU.max)
                last.then_inc(s["ml_e"], 1)
                dve.wait_ge(s["ml_exp"], h + 1)
                for lo, hi, r in ((0, WS0 + WS1, P), (WS0 + WS1, PW_, TL)):
                    last = V.scalar_tensor_tensor(P2[0:r, h % 2, lo:hi], E2[0:r, h % 2, lo:hi],
                                                  float(MLQ) ** -0.5, pb[0][0:r, lo:hi], ALU.mult, ALU.mult)
                step.link(last)
                V.tensor_tensor(P2[:, h % 2, 0:WS0 + WS1], P2[:, h % 2, 0:WS0 + WS1],
                                mcaus[:, 0:WS0 + WS1], ALU.mult)
                V.tensor_tensor(P2[0:TL, h % 2, WS0 + WS1:PW_], P2[0:TL, h % 2, WS0 + WS1:PW_],
                                mcaus[0:TL, WS0 + WS1:PW_], ALU.mult).then_inc(s["ml_pt"], 1)
                dve.wait_ge(s["ml_o"], h + 1)
                dve.wait_ge(s["ml_abs"], h + 1)
                step.link(V.tensor_tensor(mden[:, :], mden[:, :], pb[4][:, 0:T], ALU.max))
                step.link(V.reciprocal(mden[:, :], mden[:, :]))
                last = V.tensor_tensor(W[1][:, h, :], mden[:, :], pb[2][:, 0:T], ALU.mult)
                last.then_inc(s["ml_h"], 1)
            group_norm(lambda c: proj[:, HQ + c, :], lambda c: proj[:, HQ + c, :],
                       lambda c: proj[:, HG_ + c, :], 4, 1, PH_).then_inc(s["hg_done"], 1)
            group_norm(lambda c: W[1][:, c, :], lambda c: W[1][:, c, :],
                       lambda c: proj[:, MO + c, :], 4, 1, PL).then_inc(s["norm_done"], 1)

            with dve.Fori(0, 4) as i:
                for b in range(4):
                    dve.wait_ge(s["in_tile"], i * 4 + (4 * 13 + b + 1))
                    v = hT[:, bass.ds(i * 4 + b, 1), :].rearrange("p a t -> p (a t)")
                    V.tensor_tensor(v, v, pb[b][:, 0:T], ALU.add).then_inc(s["in_ev"], 1)
            dve.wait_ge(s["rs2"], 1)
            for k in range(KD):
                V.scalar_tensor_tensor(uT[:, k, :], hT[:, k, :], par[:, PF + k:PF + k + 1], Rb[:, :],
                                       ALU.mult, ALU.mult).then_inc(s["u2T_ready"], 1)
            routing(dve, V, step)

            def expert(n, wcol):
                dve.wait_ge(s["xT_ps"], n + 1)
                V.tensor_copy(xsT[:, 4:8, :, :].rearrange("p c h s -> p (c h s)"), pb[1][:, :]).then_inc(
                    s["xT_ev2"], 1)
                dve.wait_ge(s["silu_ev"], n + 1)
                V.tensor_tensor(hTb, ssb, hid_ps[:, :, CAP:2 * CAP], ALU.mult).then_inc(s["hT_ready"], 1)
                dve.wait_ge(s["y_ps"], n + 2)
                dve.wait_ge(s["y_free"], n + 1)
                V.tensor_scalar(ysb[:, 512:1024], pb[5][:, :], wcol, None, ALU.mult).then_inc(s["y_dve"], 1)

            with dve.Fori(0, NE) as i:
                expert(i, idx_base[:, 2, bass.ds(i, 1)])
            dve.wait_ge(s["ov_ready"], 1)
            count = dve.value_load(ov_n[0:1, 0:1], min_val=0, max_val=NOV)
            with dve.If(count > 0):
                with dve.Fori(0, count) as i:
                    expert(i + NE, ov_w[:, bass.ds(i, 1)])

            dve.wait_ge(s["h2_ev"], 8)
            dve.wait_ge(s["yt_in"], 32)
            for tb in range(2):
                y = slot(tb).rearrange("p (j d) -> p j d", j=2)
                step.link(V.tensor_tensor(h2[:, tb, :], h2[:, tb, :], y[:, 0, :], ALU.add))
                V.tensor_tensor(h2[:, tb, :], h2[:, tb, :], y[:, 1, :], ALU.add).then_inc(s["f_sum"], 1)
            dve.wait_ge(s["fw_in"], 16)
            for tb in range(2):
                dve.wait_ge(s["f_rs"], tb + 1)
                V.scalar_tensor_tensor(slot(tb)[:, 0:D], h2[:, tb, :], frs[:, tb:tb + 1], fw,
                                       ALU.mult, ALU.mult).then_inc(s["f_done"], 1)

        @block.tensor
        def _(pe):
            V = nc.tensor

            def product(outs, pairs, start=True, stop=True):
                n = len(pairs)
                for j, (a, b) in enumerate(pairs):
                    last = V.matmul(outs, a, b, start=start and j == 0, stop=stop and j == n - 1)
                return last

            pe.wait_ge(s["consts"], 1)
            pe.wait_ge(s["par_in"], PAR_DMAS * 16)
            V.transpose(pb[7][:, 0:P], par_rows[:, :], ident[:, :])
            V.transpose(pb[7][:, P:P + 4], lb_rows[0:4, :], ident[0:4, 0:4]).then_inc(s["par_T"], 1)
            pe.wait_ge(s["x_in"], 64)
            pe.wait_ge(s["diag_ready"], 1)
            for a, (t, n) in enumerate(TT):
                last = V.matmul(pb[6][:, t:t + n], ones[0:n, 0:P], dg[0:n, a, 0:n], start=True, stop=True)
            last.then_inc(s["R_ready"], 1)
            for k in range(KD):
                if k >= 4:
                    pe.wait_ge(s["x_ev"], k - 3)
                for a, (t, n) in enumerate(TT):
                    last = V.transpose(pb[k % 4][:, t:t + n], xin[0:n, a, k * P:(k + 1) * P], ident[0:n, 0:n])
                last.then_inc(s["x_T"], 1)

            pe.wait_ge(s["uT_ready"], KD)
            pe.wait_ge(s["gatew_in"], 32)
            product(pb[4][0:MLH, 0:T], [(wg[:, k, 0:MLH], uT[:, k, :]) for k in range(KD)]).then_inc(s["gi_ready"], 1)
            product(pb[5][0:NFD, 0:T], [(wg[:, k, MLH:NG], uT[:, k, :]) for k in range(KD)]).then_inc(s["gf_ready"], 1)

            def project(passes, base, rhs):
                with pe.Fori(0, passes) as i:
                    for a, landed in enumerate((s["in_a"], s["in_b"])):
                        pe.wait_ge(landed, i * 16 + (base + 1) * 16)
                        for b in range(2):
                            pe.wait_ge(s["in_ev"], i * 4 + (4 * base + 2 * a + b + 1))
                            product(pb[2 * a + b][:, 0:T],
                                    [(wchunk(a)[:, k, b * P:(b + 1) * P], rhs(k)) for k in range(KD)]).then_inc(
                                        s["in_tile"], 1)

            def uT_k(k):
                return uT[:, k, :]

            project(6, 0, uT_k)
            pe.wait_ge(s["g_rows"], 1)
            for a, (t, n) in enumerate(TT):
                V.transpose(pb[6][0:n, 64 * a:64 * a + NFD], gX[:, t:t + n], ident[0:NFD, 0:NFD])
                V.transpose(pb[6][0:n, 64 * a + NFD:64 * a + 2 * NFD], gA[:, t:t + n], ident[0:NFD, 0:NFD])
                last = V.transpose(pb[6][0:n, 64 * a + 2 * NFD:64 * a + 2 * NFD + MLH], gL[:, t:t + n],
                                   ident[0:MLH, 0:MLH])
            last.then_inc(s["g_col"], 1)
            project(4, 6, uT_k)

            pe.wait_ge(s["conv_done"], 16 + 4)
            for g in range(SSG):
                for c, a, t, n in SC:
                    r = TT[a][1]
                    last = V.matmul(pb[4 + g][0:r, c:c + n], proj[:, B0 + g, TT[a][0]:TT[a][0] + r],
                                    proj[:, C0 + g, t:t + n], start=True, stop=True)
                last.then_inc(s["cb_ready"], 1)

            def by_token(dst_bank, tile0, tiles, a):
                t, n = TT[a]
                for j in range(tiles):
                    last = V.transpose(dst_bank[0:n, j * P:(j + 1) * P], proj[:, tile0 + j, t:t + n], ident[:, :])
                return last

            pe.wait_ge(s["in_ev"], 4 * 10 + 4)
            for a in range(NT):
                for hf_ in range(2):
                    m = 2 * a + hf_
                    if m >= 4:
                        pe.wait_ge(s["xv_ev"], m - 3)
                    by_token(pb[m % 4], X0 + 4 * hf_, 4, a).then_inc(s["xv_T"], 1)
            pe.wait_ge(s["xv_ev"], 2 * NT)

            def row(bank, r, rows, src):
                return V.matmul(bank[:, 0:T], sel[0:rows, r, :], src[0:rows, :], start=True, stop=True)

            def causal(out_, v, scores):
                for j, (c, a, t, n) in enumerate(SC):
                    r = TT[a][1]
                    last = V.matmul(out_[:, t:t + n], v(a, r), scores(r, c, n), start=j == 0, stop=j == NT - 1)
                return last

            def ssm_row(e):
                if e >= 2:
                    pe.wait_ge(s["e_ready"], e - 1)
                row(pb[e % 2], MLH + e, NFD, gX).then_inc(s["bc_ready"], 1)

            ssm_row(0)
            ssm_row(1)
            for e in range(SSH):
                pe.wait_ge(s["pt_ready"], e + 1)
                if e >= 4 and e % 2 == 0:
                    pe.wait_ge(s["y_ev"], e // 2 - 1)
                q = 64 * (e % 2)
                causal(pb[2 + (e // 2) % 2][q:q + 64, :],
                       lambda a, r: xv[0:r, a, e * 64:(e + 1) * 64],
                       lambda r, c, n: P2[0:r, e % 2, c:c + n]).then_inc(s["y_ready"], 1)
                if e + 2 < SSH:
                    ssm_row(e + 2)

            norm_no = [0]

            def norm_sums(sq, groups, tiles, banks):
                pe.wait_ge(s["sq_ready"], norm_no[0] + 1)
                for g in range(groups):
                    product(pb[banks + g][:, 0:T],
                            [(ones[:, 0:P], sq[:, g * tiles + j, :]) for j in range(tiles)]).then_inc(s["sum_ready"], 1)
                norm_no[0] += 1

            norm_sums(sq8, 4, 2, 4)
            project(3, 10, uT_k)

            pe.wait_ge(s["rs_ready"], 1)
            for m, tile0 in enumerate((HV, MV)):
                for a in range(NT):
                    c = 3 * m + a
                    pe.wait_ge(s["in_ev"], tile0 + 4 + 4)
                    if c >= 2:
                        pe.wait_ge(s["hv_ev"], c - 1)
                    by_token(pb[6 + c % 2], tile0, 4, a).then_inc(s["hv_T"], 1)

            pe.wait_ge(s["hlin"], 1)
            pe.wait_ge(s["in_ev"], 4 * 13 + 4)
            for l in range(-1, NLEV):
                if l >= 0:
                    pe.wait_ge(s["lv_w"], l + 1)
                if l >= 1:
                    pe.wait_ge(s["lv_ev"], l)
                b = 3 * ((l + 1) % 2)
                ks = proj[:, HF:HF + 4, :] if l < 0 else W[l % 2]
                qs = proj[:, HQ:HQ + 4, :] if l < 0 else W[l % 2]
                for h in range(HGH):
                    if l < 7:
                        for a in range(2):
                            last = V.matmul(pb[b + a][:, h * P:(h + 1) * P], ks[:, h, a * P:(a + 1) * P],
                                            qs[:, h, a * P:(a + 1) * P], start=True, stop=True)
                        if l < 0 or LH[l] <= 8:
                            last = V.matmul(pb[b + 2][0:TL, h * TL:(h + 1) * TL], ks[:, h, 2 * P:T],
                                            qs[:, h, 2 * P:T], start=True, stop=True)
                    elif l == 7:
                        last = V.matmul(pb[b][:, h * P:(h + 1) * P], ks[:, h, 0:P], qs[:, h, P:2 * P],
                                        start=True, stop=True)
                    else:
                        for a in range(2):
                            last = V.matmul(pb[b][:, (4 * a + h) * TL:(4 * a + h + 1) * TL],
                                            ks[:, h, a * P:(a + 1) * P], qs[:, h, 2 * P:T],
                                            start=True, stop=True)
                last.then_inc(s["lvd_ps"] if l < 0 else s["lv_ps"], 1)
            pe.wait_ge(s["lv_ev"], NLEV + 1)
            pe.wait_ge(s["hv_ev"], 2 * NT)
            for h in range(HGH):
                if h >= 2:
                    pe.wait_ge(s["ho_ev"], h - 1)
                causal(pb[4 + h % 2], lambda a, r: hv[0:r, a, h * P:(h + 1) * P],
                       lambda r, c, n: PHs[0:r, h, c:c + n]).then_inc(s["ho_ps"], 1)

            pe.wait_ge(s["ho_ev"], HGH)
            for h in range(MLH):
                q = 64 * (h % 2)
                if h >= 1:
                    pe.wait_ge(s["ml_pt"], h)
                for c, a, t, n in SC:
                    r = TT[a][1]
                    last = V.matmul(pb[0][0:r, c:c + n], proj[q:q + 64, MK + h // 2, TT[a][0]:TT[a][0] + r],
                                    proj[q:q + 64, MQ + h // 2, t:t + n], start=True, stop=True)
                row(pb[1], h, MLH, gG).then_inc(s["ml_ps"], 1)
                if h >= 1:
                    pe.wait_ge(s["ml_h"], h)
                row(pb[4], h, MLH, gZ)
                pe.wait_ge(s["ml_pt"], h + 1)
                causal(pb[2], lambda a, r: mv[0:r, a, h * P:(h + 1) * P],
                       lambda r, c, n: P2[0:r, h % 2, c:c + n])
                causal(pb[3], lambda a, r: ones[0:r, 0:P],
                       lambda r, c, n: P2[0:r, h % 2, c:c + n]).then_inc(s["ml_o"], 1)
            norm_sums(sqH, 4, 1, 4)
            norm_sums(sqH, 4, 1, 4)

            pe.wait_ge(s["norm_done"], 1)
            for j in (0, 1, 2, 4):
                pe.sem_inc(m_free[j], 1)
            pe.sem_inc(s["h_ps"], 1)
            pe.sem_inc(s["y_ps"], 1)
            project(4, 13, lambda k: proj[:, MIXED[k], :])

            for k in range(KD):
                pe.wait_ge(s["sq2"], k + 1)
                last = V.matmul(pb[4][:, 0:T], ones[:, 0:P], uT[:, k, :], start=k == 0, stop=k == KD - 1)
            last.then_inc(s["sum2"], 1)
            pe.wait_ge(s["routerw_in"], 80)
            pe.wait_ge(s["u2T_ready"], KD)
            for a, (t, n) in enumerate(TT):
                last = product(pb[5][0:n, a * LG:(a + 1) * LG],
                               [(uT[:, k, t:t + n], wr[:, k, :]) for k in range(KD)])
            last.then_inc(s["lg_ready"], 1)
            for a, (t, n) in enumerate(TT):
                for q in range(4):
                    if a >= 1:
                        pe.wait_ge(s["t_ev"], 4 * a + q - 3)
                    for j in range(4):
                        last = V.transpose(pb[q][0:n, j * P:(j + 1) * P], uT[:, 4 * q + j, t:t + n], ident[:, :])
                    last.then_inc(s["t_ps"], 1)
            pe.wait_ge(s["pairs"], 1)
            for a, (t, n) in enumerate(TT):
                product(pb[6][0:n, a * NE:(a + 1) * NE],
                        [(ones[:, 0:n], chosen[:, j, :]) for j in range(a)]
                        + [(before[0:n, 0:n], chosen[0:n, a, :])])
            product(pb[6][:, NT * NE:(NT + 1) * NE],
                    [(ones[0:n, 0:P], chosen[0:n, a, :]) for a, (t, n) in enumerate(TT)]).then_inc(s["ranks"], 1)
            for m in range(2 * NT):
                n = TT[m // 2][1]
                pe.wait_ge(s["rhs_ready"], m + 1)
                last = V.matmul(pb[7][:, 0:3 * NC_], slot_hot[m % 2][0:n, :],
                                rhs_t[m % 2][0:n, :, :].rearrange("p a c -> p (a c)"),
                                start=m == 0, stop=m == 2 * NT - 1)
                last.then_inc(s["rhs_used"], 1)
            pe.wait_ge(s["t_ev"], 12)
            pe.wait_ge(s["idx_ready"], 1)
            for tb in range(2):
                for q in range(4):
                    for j in range(4):
                        last = V.transpose(pb[4 * tb + q][:, j * P:(j + 1) * P],
                                           hT[:, 4 * q + j, NM + tb * P:NM + (tb + 1) * P], ident[:, :])
                    last.then_inc(s["h2_ps"], 1)
            pe.wait_ge(s["h2_ev"], 8)

            def expert(n, landed_rows):
                pe.wait_ge(s["xs_in"], landed_rows)
                for c in range(8):
                    last = V.transpose(pb[c // 4][:, (c % 4) * P:(c % 4 + 1) * P], xs[:, c * P:(c + 1) * P],
                                       ident[:, :])
                last.then_inc(s["xT_ps"], 1)
                pe.wait_ge(s["xT_ev"], n + 1)
                pe.wait_ge(s["xT_ev2"], n + 1)
                for hf_ in range(2):
                    pe.wait_ge(m_in[2 * hf_], n * 16 + 16)
                    pe.wait_ge(m_in[2 * hf_ + 1], n * 16 + 16)
                    for c in range(8):
                        for g in range(2):
                            w = slot((2 * hf_ + g + 2) % 6).rearrange("p (k f) -> p k f", f=FE)
                            last = V.matmul(pb[2][64 * g:64 * g + 64, :], xsT[:, c, hf_, :], w[:, c, :],
                                            start=hf_ + c == 0, stop=hf_ == 1 and c == 7)
                            if c == 7:
                                last.then_inc(s["h_ps"] if hf_ and g else m_free[2 * hf_ + g], 1)
                pe.wait_ge(s["h_ev"], n + 1)
                for k in range(KF):
                    last = V.transpose(pb[3][:, k * P:(k + 1) * P], hs[:, k * P:(k + 1) * P], ident[:, :])
                last.then_inc(s["hT_ps"], 1)
                pe.wait_ge(s["hT_ready"], n + 1)
                pe.wait_ge(s["y_free"], n + 1)
                for k in range(KF):
                    if k % 2 == 0:
                        pe.wait_ge(m_in[4 + k // 2], n * 16 + 16)
                    w = slot(k // 2).rearrange("p (k d) -> p k d", d=D)
                    for d in range(2):
                        for g in range(2):
                            last = V.matmul(pb[4 + d][64 * g:64 * g + 64, :], hTb[:, k, :],
                                            w[:, k % 2, g * 1024 + d * 512:g * 1024 + (d + 1) * 512],
                                            start=k == 0, stop=k == KF - 1)
                    if k == 1:
                        last.then_inc(m_free[4], 1)
                last.then_inc(s["y_ps"], 1)

            with pe.Fori(0, NE) as i:
                expert(i, i * 16 + 16)
            pe.wait_ge(s["ov_ready"], 1)
            count = pe.value_load(ov_n[0:1, 0:1], min_val=0, max_val=NOV)
            with pe.If(count > 0):
                with pe.Fori(0, count) as i:
                    expert(i + NE, i * 16 + (NE + 2) * 16)


_INS = ['x', 'meta_tokens', 'hg_lb_logits', 'norm_mix_w', 'w_in', 'hg_norm_w', 'ml_b_i', 'ml_b_f', 'ml_norm_w',
        'ssm_conv_w', 'ssm_conv_b', 'ssm_dt_bias', 'ssm_a_log', 'ssm_d', 'ssm_norm_w', 'w_out', 'norm_ffn_w',
        'moe_w_group', 'moe_b_group', 'moe_w_router', 'moe_b_router', 'moe_w1', 'moe_w3', 'moe_w2', 'final_norm_w']
_OUTS = [((1, 256, 2048), 'float32')]


def kernel(**inputs):
    import numpy as _np
    import concourse.bacc as _bacc
    from concourse import mybir as _mybir
    from concourse.bass_utils import run_bass_kernel_spmd as _run

    nc = _bacc.Bacc("TRN2", target_bir_lowering=False, num_devices=1)
    arrays, args = {}, []
    for name in _INS:
        a = _np.ascontiguousarray(inputs[name])
        arrays[f"in_{name}_dram"] = a
        args.append(nc.dram_tensor(f"in_{name}_dram", a.shape, _mybir.dt.from_np(a.dtype), kind="ExternalInput").ap())
    for i, (shape, dtype) in enumerate(_OUTS):
        dt = _mybir.dt.from_np(_np.dtype(dtype))
        args.append(nc.dram_tensor(f"out_{i}_dram", shape, dt, kind="ExternalOutput").ap())
    hymba_moe_layer(nc, *args)
    r = _run(nc, [arrays], core_ids=[0])
    return r.results[0]["out_0_dram"]
```

```python
import numpy as np
import concourse.bass as bass
from concourse import mybir
from contextlib import ExitStack


class Steps:

    def __init__(self, eng, sem):
        self.eng, self.sem, self.n, self.reg, self.per = eng, sem, 0, None, 0

    def link(self, ins):
        ins.then_inc(self.sem, 1)
        self.n += 1
        self.eng.wait_ge(self.sem, self.n if self.reg is None else self.reg * self.per + self.n)

    def enter(self, reg, per):
        self.reg, self.per, self.before = reg, per, self.n

    def leave(self, passes):
        assert self.n - self.before == self.per, (self.n - self.before, self.per)
        self.n = self.before + self.per * passes
        self.reg = None


def hymba_moe_layer(nc, x, meta_tokens, hg_lb_logits, norm_mix_w, w_in, hg_norm_w, ml_b_i, ml_b_f,
                    ml_norm_w, ssm_conv_w, ssm_conv_b, ssm_dt_bias, ssm_a_log, ssm_d, ssm_norm_w,
                    w_out, norm_ffn_w, moe_w_group, moe_b_group, moe_w_router, moe_b_router,
                    moe_w1, moe_w3, moe_w2, final_norm_w, out):
    f32 = mybir.dt.float32
    i32 = mybir.dt.int32
    u32 = mybir.dt.uint32
    ALU = mybir.AluOpType
    ACT = mybir.ActivationFunctionType
    AX = mybir.AxisListType

    P = 128
    D = x.shape[2]
    NM = meta_tokens.shape[0]
    SEQ = x.shape[1]
    T = NM + SEQ
    KD = D // P
    TT = [(t, min(P, T - t)) for t in range(0, T, P)]
    NT = len(TT)
    TL = TT[-1][1]
    EPS = 1e-6
    HGH, MLH, SSH, SSG = 4, ml_b_i.shape[1], ssm_d.shape[1], 4
    MLQ = 64
    CONVW = ssm_conv_w.shape[1]
    GRP, EPG = moe_w_router.shape[1], moe_w_router.shape[3]
    NE = GRP * EPG
    FE = moe_w1.shape[3]
    KF = FE // P
    CAP = 64
    NB = -(-T // CAP)
    NOV = (2 * T) // (CAP + 1)
    NC_ = NB * NE

    C_IF = 3584
    C_Z = C_IF + 2 * MLH
    C_DT = C_Z + 3072
    CH = 256
    IG0 = 32
    NFD = MLH + SSH

    Z0, X0, B0, C0 = 0, 8, 16, 20
    HQ, HF, HV, HG_, MQ, MK, MV, MO = 24, 28, 32, 36, 40, 42, 44, 48
    NP_ = 52
    MIXED = [HG_ + i for i in range(4)] + [MO + i for i in range(4)] + [Z0 + i for i in range(8)]

    PM, PF, PH_, PL, PS, PW, PB = 0, 16, 32, 36, 40, 48, 112

    SLOT = 4096
    NSLOT = 6
    WS0, WS1, WD = 272, 144, TL
    PW_ = WS0 + WS1 + WD

    ctx = ExitStack()
    with ctx:
        def sb(name, shape, dt=f32):
            return ctx.enter_context(nc.sbuf_tensor(name, shape, dt))

        def sem(name):
            return ctx.enter_context(nc.semaphore(name))

        ring = sb("ring", [P, NSLOT * SLOT])
        hT = sb("hT", [P, KD, T])
        uT = sb("uT", [P, KD, T])
        proj = sb("proj", [P, NP_, T])
        pflat = proj[:, :, :].rearrange("p a t -> p (a t)")

        def slot(j):
            return ring[:, j * SLOT:(j + 1) * SLOT]

        def wchunk(j):
            return slot(j).rearrange("p (k c) -> p k c", k=KD)

        xin = ring[:, 4 * SLOT:4 * SLOT + NT * D].rearrange("p (a d) -> p a d", a=NT)
        at = [2 * SLOT]

        def scr(n):
            at[0] += n
            assert at[0] <= NSLOT * SLOT
            return ring[:, at[0] - n:at[0]]

        sel = scr(NFD * P).rearrange("p (r c) -> p r c", r=NFD)
        EPb = scr(4 * PW_)
        E2 = EPb[:, 0:2 * PW_].rearrange("p (a c) -> p a c", a=2)
        P2 = EPb[:, 2 * PW_:4 * PW_].rearrange("p (a c) -> p a c", a=2)
        cumT = EPb[:, 0:4 * T].rearrange("p (h t) -> p h t", h=4)
        CBr = scr(4 * PW_)
        CB = CBr.rearrange("p (g c) -> p g c", g=4)
        rs4 = CBr[:, 0:4 * T].rearrange("p (h t) -> p h t", h=4)
        xv = scr(NT * 1024).rearrange("p (a c) -> p a c", a=NT)
        hv = scr(NT * 512).rearrange("p (a c) -> p a c", a=NT)
        mv = scr(NT * 512).rearrange("p (a c) -> p a c", a=NT)
        PHs = scr(4 * PW_).rearrange("p (h c) -> p h c", h=4)
        Wb = scr(2 * 4 * T)
        mden = Wb[:, 0:T]
        W = [Wb[:, i * 4 * T:(i + 1) * 4 * T].rearrange("p (h t) -> p h t", h=4) for i in range(2)]
        sq8 = Wb.rearrange("p (h t) -> p h t", h=8)
        conv = [Wb[:, i * T:(i + 1) * T] for i in range(4)]
        sqH = EPb[:, 0:4 * T].rearrange("p (h t) -> p h t", h=4)

        ident = sb("ident", [P, P])
        ones = sb("ones", [P, T])
        before = sb("before", [P, P])
        mcaus = sb("mcaus", [P, PW_])
        LV = [1, 2, 4, 8, 16, 32, 64]
        mlev = sb("mlev", [P, len(LV), P])
        par_rows = CBr[:, 0:P]
        lb_rows = CBr[:, P:2 * P]
        epsc = sb("epsc", [P, 1])
        fss = sb("fss", [P, 2])
        frs = sb("frs", [P, 2])
        par = sb("par", [P, P + 4])
        lb4 = sb("lb4", [P, 4, 4])
        wg = sb("wg", [P, KD, IG0 + MLH])
        wr = sb("wr", [P, KD, 36])
        brow = sb("brow", [P, 36])
        dB = sb("dB", [P, SSH])
        dcol = sb("dcol", [P, SSH // 2])
        gcols = sb("gcols", [NFD, 4])
        ss3 = sb("ss3", [P, NT])
        rs3 = sb("rs3", [P, NT])
        dg = EPb[:, 0:NT * P].rearrange("p (a c) -> p a c", a=NT)
        Rb = sb("Rb", [P, T])
        gX = sb("gX", [NFD, T])
        gA = hv[0:NFD, 0, 0:T]
        gZ = sb("gZ", [NFD, T])
        gQ = hv[0:NFD, 1, 0:T]
        gL = hv[0:MLH, 2, 0:T]
        gG = sb("gG", [MLH, T])
        colc = sb("colc", [P, NT, 2 * NFD + MLH])

        pb = [ctx.enter_context(nc.psum_tensor(f"bank{i}", [P, 512], f32)) for i in range(8)]

        moff = [0]

        def mo(n):
            moff[0] += n
            assert moff[0] <= NP_ * T
            return pflat[:, moff[0] - n:moff[0]]

        sqk = proj[:, X0:X0 + 8, :]
        sqa = proj[:, B0, :]
        lgT = proj[:, B0 + 1, :]
        u2 = mo(NT * D).rearrange("p (a d) -> p a d", a=NT)
        h2 = pflat[:, 0:2 * D].rearrange("p (a d) -> p a d", a=2)
        xs = mo(1024)
        xsT = mo(1024).rearrange("p (c h s) -> p c h s", c=8, h=2)
        hs = mo(512)
        ssb = mo(KF * CAP).rearrange("p (k s) -> p k s", k=KF)
        hTb = mo(KF * CAP).rearrange("p (k s) -> p k s", k=KF)
        ysb = mo(1024)
        fw = uT[:, 0:8, :].rearrange("p k t -> p (k t)")[:, 0:D]
        hid_ps = pb[3][:, :].rearrange("p (k c) -> p k c", k=KF)
        rat = [moff[0]]

        def ro(n):
            rat[0] += n
            assert rat[0] <= NP_ * T
            return pflat[:, rat[0] - n:rat[0]]

        idx_base = sb("idx_base", [P, 3, NC_])
        idx_x = sb("idx_x", [P, NC_], i32)
        idx_y = sb("idx_y", [P, NC_], i32)
        ov_x = sb("ov_x", [P, NOV], i32)
        ov_y = sb("ov_y", [P, NOV], i32)
        ov_w = sb("ov_w", [P, NOV])
        ov_e = sb("ov_e", [P, NOV], i32)
        ov_n = sb("ov_n", [P, 1], i32)
        xcol = sb("xcol", [P, 1], i32)
        ycol = sb("ycol", [P, 1], i32)

        u2d = nc.dram_tensor("tokens_normed", (2 * T, 1024), f32, kind="Internal").ap()
        yd = nc.dram_tensor("expert_rows", (4 * T, 1024), f32, kind="Internal").ap()

        LH = LV + [P, 2 * P]
        NLEV = len(LH)
        LWID = [T if h <= 8 or h == 2 * P else 2 * P for h in LH]
        PAR_DMAS = 11
        HEADS_AT = [[e for e in range(SSH) if 3 + e * 12 // SSH == u] for u in range(16)]
        LEVELS_AT = [[-1, 0], [1, 2], [3, 4], [5, 6], [7, 8]]

        s = {n: sem(n) for n in (
            "lg_T rs2 iotas gmax pairs ranks gmax_e rhs_used rhs_ready idx_ready ov_ready gatew_in "
            "par_in routerw_in in_a in_b in_ev h_ps y_ps y_out f_done out_sem pool_steps "
            "ident_ready consts pool_waited xT_ps col_x xs_in col_y y_act y_dve ys_out y_free "
            "u2_out act_steps conv_done params_zeroed rms_ready gate_cols_in lb_diff lb_exp "
            "alog_exp gf_ready gcols_ready li_ready fd_x fd_tanh fd_e em_t em_exp in_tile conv_acc "
            "xv_T xv_ev e_ready e_exp sq_ready sum_ready rs_ready ssm_gated hsig hg_gate hlin hln "
            "hv_T hv_ev lv_d lv_e ml_e ml_exp ml_o ml_abs ml_h mo_gate hg_done sq_acc sq2 "
            "u2T_ready sum2 t_ps t_ev h2_ps h2_ev fw_in xT_ev h_ev hT_ps silu_ev f_sum f_rs "
            "dve_steps x_T x_ev par_T par_ev diag_ready R_ready uT_ready g_rows g_col g_colev "
            "cb_ready cb_ev bc_ready y_ready pt_ready y_ev lv_ps lv_w lvd_ps lv_ev ho_ps ho_ev "
            "ml_ps ml_pt norm_done lg_ready lg_ev xT_ev2 hT_ready"
        ).split()}
        X_IN = [(sem(f"tokens_in{a}"), 2 if a == 0 else 1) for a in range(NT)]
        yt_in = [[sem(f"token_rows_in{tb}_{j}") for j in range(2)] for tb in range(2)]
        m_in = [sem(f"expert_in{j}") for j in range(NSLOT)]
        m_free = {j: sem(f"expert_free{j}") for j in (0, 1, 2, 4)}

        LG = GRP + NE
        io_e = ro(NE)
        io_s = ro(P)
        io_t = ro(2 * NT).rearrange("p (a j) -> p a j", j=2)
        io_c = ro(NC_ - NE)
        half = ro(1)
        L = ro(NT * LG).rearrange("p (a c) -> p a c", a=NT)
        rt_ex = ro(NT * 5).rearrange("p (a c) -> p a c", a=NT)
        g8, e8, mg, me_ = (ro(NT * 8).rearrange("p (a c) -> p a c", a=NT) for _ in range(4))
        ig, ie = (ro(NT * 8).bitcast(u32).rearrange("p (a c) -> p a c", a=NT) for _ in range(2))
        igf, gsum, wden = (ro(NT).rearrange("p (a c) -> p a c", a=NT) for _ in range(3))
        ief, w01, rankj, blk, slj, tj = (ro(NT * 2).rearrange("p (a c) -> p a c", a=NT) for _ in range(6))
        ohg = ro(NT * GRP).rearrange("p (a c) -> p a c", a=NT)
        esel = ro(NT * NE).rearrange("p (a g e) -> p a g e", a=NT, g=GRP)
        OH = ro(NT * 2 * NE).rearrange("p (a j e) -> p a j e", a=NT, j=2)
        rk2 = ro(NT * 2 * NE).rearrange("p (a j e) -> p a j e", a=NT, j=2)
        chosen = ro(NT * NE).rearrange("p (a e) -> p a e", a=NT)
        rankt = ro((NT + 1) * NE).rearrange("p (a e) -> p a e", e=NE)
        hot5 = ro(NT * 2 * NB).rearrange("p (a j b) -> p a j b", a=NT, j=2)
        slot_hot = [ro(P) for _ in range(2)]
        rhs_t = [ro(3 * NC_).rearrange("p (a c) -> p a c", a=3) for _ in range(2)]
        unused = ro(NC_)
        tmpc = ro(NC_)
        idxf = ro(2 * NC_).rearrange("p (a c) -> p a c", a=2)
        F_ = ro(NC_ - NE)
        O_ = ro(NC_ - NE)
        S_ = ro(NC_ - NE)
        Sj = ro(NC_ - NE)
        ovf = ro(4 * NOV).rearrange("p (a c) -> p a c", a=4)

        def routing(dve, V, step):
            def bc(ap, shape):
                return ap.to_broadcast(shape)

            V.memset(L, 0.0)
            V.memset(g8, -3e38)
            step.link(V.memset(rankt, 0.0))
            dve.wait_ge(s["lg_T"], 1)
            dve.wait_ge(s["rs2"], 1)
            for a, (_, n) in enumerate(TT):
                last = V.scalar_tensor_tensor(L[0:n, a, :], pb[5][0:n, a * LG:(a + 1) * LG], rs3[0:n, a:a + 1],
                                              brow[0:n, :], ALU.mult, ALU.add)
            step.link(last)
            step.link(V.tensor_copy(g8[:, :, 0:GRP], L[:, :, 0:GRP]))
            for a in range(NT):
                last = V.max(mg[:, a, :], g8[:, a, :])
            step.link(last)
            for a in range(NT):
                last = V.max_index(ig[:, a, :], mg[:, a, :], g8[:, a, :])
            step.link(last)
            step.link(V.tensor_copy(igf, ig[:, :, 0:1]))
            V.tensor_tensor(rt_ex[:, :, 0:GRP], L[:, :, 0:GRP], bc(mg[:, :, 0:1], [P, NT, GRP]), ALU.subtract)
            dve.wait_ge(s["iotas"], 1)
            step.link(V.tensor_tensor(ohg, io_e[:, 0:GRP].unsqueeze(1).to_broadcast([P, NT, GRP]),
                                      bc(igf, [P, NT, GRP]), ALU.is_equal))
            step.link(V.tensor_tensor(esel, L[:, :, GRP:LG].rearrange("p a (g e) -> p a g e", g=GRP),
                                      ohg.unsqueeze(3).to_broadcast([P, NT, GRP, EPG]), ALU.mult))
            step.link(V.tensor_reduce(e8, esel.rearrange("p a g e -> p a e g"), AX.X, ALU.add))
            for a in range(NT):
                last = V.max(me_[:, a, :], e8[:, a, :])
            step.link(last)
            for a in range(NT):
                V.max_index(ie[:, a, :], me_[:, a, :], e8[:, a, :])
            V.tensor_tensor(rt_ex[:, :, GRP:GRP + 1], me_[:, :, 1:2], me_[:, :, 0:1], ALU.subtract).then_inc(s["gmax"], 1)
            dve.wait_ge(s["gmax"], 1)
            step.link(V.tensor_copy(ief, ie[:, :, 0:2]))
            step.link(V.scalar_tensor_tensor(ief, bc(igf, [P, NT, 2]), float(EPG), ief, ALU.mult, ALU.add))
            for j in range(2):
                last = V.tensor_tensor(OH[:, :, j, :], io_e[:, 0:NE].unsqueeze(1).to_broadcast([P, NT, NE]),
                                       bc(ief[:, :, j:j + 1], [P, NT, NE]), ALU.is_equal)
            step.link(last)
            V.tensor_tensor(chosen, OH[:, :, 0, :], OH[:, :, 1, :], ALU.add).then_inc(s["pairs"], 1)
            dve.wait_ge(s["ranks"], 1)
            for a, (_, n) in enumerate(TT):
                V.tensor_copy(rankt[0:n, a, :], pb[6][0:n, a * NE:(a + 1) * NE])
            step.link(V.tensor_copy(rankt[:, NT, :], pb[6][:, NT * NE:(NT + 1) * NE]))
            for j in range(2):
                last = V.tensor_tensor(rk2[:, :, j, :], OH[:, :, j, :], rankt[:, 0:NT, :], ALU.mult)
            step.link(last)
            step.link(V.tensor_reduce(rankj, rk2, AX.X, ALU.add))
            step.link(V.tensor_scalar(blk, rankj, float(CAP), None, ALU.is_ge))
            for b in range(2, NB):
                step.link(V.scalar_tensor_tensor(blk, rankj, float(CAP * b), blk, ALU.is_ge, ALU.add))
            V.scalar_tensor_tensor(slj, blk, -float(CAP), rankj, ALU.mult, ALU.add)
            V.tensor_scalar(tj, io_t, 1.0, None, ALU.add)
            for j in range(2):
                last = V.tensor_tensor(hot5[:, :, j, :], io_e[:, 0:NB].unsqueeze(1).to_broadcast([P, NT, NB]),
                                       bc(blk[:, :, j:j + 1], [P, NT, NB]), ALU.is_equal)
            step.link(last)
            dve.wait_ge(s["gmax_e"], 1)
            step.link(V.tensor_reduce(gsum, rt_ex[:, :, 0:GRP], AX.X, ALU.add))
            step.link(V.scalar_tensor_tensor(wden, rt_ex[:, :, GRP:GRP + 1], 1.0, gsum, ALU.add, ALU.mult))
            step.link(V.reciprocal(w01[:, :, 0:1], wden))
            step.link(V.tensor_tensor(w01[:, :, 1:2], w01[:, :, 0:1], rt_ex[:, :, GRP:GRP + 1], ALU.mult))
            for m in range(2 * NT):
                a, j = m // 2, m % 2
                n = TT[a][1]
                if m >= 2:
                    dve.wait_ge(s["rhs_used"], m - 1)
                r = rhs_t[m % 2]
                V.tensor_scalar(slot_hot[m % 2][0:n, :], io_s[0:n, :], slj[0:n, a, j:j + 1], None, ALU.is_equal)
                step.link(V.tensor_tensor(r[0:n, 1, :].rearrange("p (b e) -> p b e", e=NE),
                                          OH[0:n, a, j, :].unsqueeze(1).to_broadcast([n, NB, NE]),
                                          hot5[0:n, a, j, :].unsqueeze(2).to_broadcast([n, NB, NE]), ALU.mult))
                V.tensor_scalar(r[0:n, 0, :], r[0:n, 1, :], tj[0:n, a, 0:1], None, ALU.mult)
                V.tensor_scalar(r[0:n, 2, :], r[0:n, 1, :], w01[0:n, a, j:j + 1], None, ALU.mult)
                V.tensor_scalar(r[0:n, 1, :], r[0:n, 1, :], tj[0:n, a, j:j + 1], None, ALU.mult).then_inc(
                    s["rhs_ready"], 1)
            dve.wait_ge(s["rhs_used"], 2 * NT)
            step.link(V.tensor_copy(idx_base[:, :, :].rearrange("p a c -> p (a c)"), pb[7][:, 0:3 * NC_]))
            step.link(V.tensor_scalar(unused, idx_base[:, 0, :], 0.5, 65536.0, ALU.is_lt, ALU.mult))
            step.link(V.tensor_scalar(unused, unused, half[:, 0:1], None, ALU.add))
            V.scalar_tensor_tensor(idxf[:, 0, :], idx_base[:, 0, :], -1.0, unused, ALU.add, ALU.add)
            step.link(V.scalar_tensor_tensor(tmpc, idx_base[:, 1, :], 2.0, unused, ALU.mult, ALU.add))
            step.link(V.tensor_scalar(idxf[:, 1, :], tmpc, -2.0, None, ALU.add))
            V.tensor_copy(idx_x[:, :], idxf[:, 0, :])
            V.tensor_copy(idx_y[:, :], idxf[:, 1, :]).then_inc(s["idx_ready"], 1)

        AHEAD = 4

        def further_passes(V, step, part):
            if part == 0:
                for b in range(1, NB):
                    last = V.tensor_scalar(F_[:, (b - 1) * NE:b * NE], rankt[:, NT, :], float(CAP * b), None,
                                           ALU.is_gt)
                step.link(last)
                step.link(V.tensor_tensor_scan(O_, ones[:, 0:NC_ - NE], F_, 0.0, ALU.mult, ALU.add))
                step.link(V.tensor_copy(ov_n[:, :], O_[:, NC_ - NE - 1:NC_ - NE]))
                step.link(V.tensor_tensor(O_, O_, F_, ALU.subtract))
            for i in range(part, NOV, AHEAD):
                step.link(V.scalar_tensor_tensor(S_, O_, float(i), F_, ALU.is_equal, ALU.mult))
                for q, src in enumerate((idxf[:, 0, NE:NC_], idxf[:, 1, NE:NC_], idx_base[:, 2, NE:NC_], io_c)):
                    step.link(V.scalar_tensor_tensor(Sj, S_, 1.0, src, ALU.mult, ALU.mult,
                                                     accum_out=ovf[:, q, i:i + 1]))
            if part == AHEAD - 1:
                V.tensor_copy(ov_x[:, :], ovf[:, 0, :])
                V.tensor_copy(ov_y[:, :], ovf[:, 1, :])
                V.tensor_copy(ov_w[:, :], ovf[:, 2, :])
                V.tensor_copy(ov_e[:, :], ovf[:, 3, :]).then_inc(s["ov_ready"], 1)

        nc_block = ctx.enter_context(nc.Block())
        block = nc_block

        SC = [(0, 0, 0, T), (WS0, 1, P, T - P), (WS0 + WS1, 2, 2 * P, TL)]

        def columns(w, c):
            return w[0, :, bass.ds(c, CH)].rearrange("(k p) c -> p k c", p=P)

        @block.sync
        def _(sp):
            sp.dma_start(xin[0:NM, 0, :], meta_tokens[:, :]).then_inc(X_IN[0][0], 16)
            sp.dma_start(xin[NM:P, 0, :], x[0, 0:P - NM, :]).then_inc(X_IN[0][0], 16)
            sp.dma_start(xin[:, 1, :], x[0, P - NM:2 * P - NM, :]).then_inc(X_IN[1][0], 16)
            sp.dma_start(xin[0:TL, 2, :], x[0, 2 * P - NM:SEQ, :]).then_inc(X_IN[2][0], 16)
            sp.dma_start(wg[:, :, IG0:IG0 + MLH],
                         w_in[0, :, C_IF:C_IF + MLH].rearrange("(k p) c -> p k c", p=P)).then_inc(s["gatew_in"], 16)
            sp.dma_start(wg[:, :, 0:MLH],
                         w_in[0, :, C_IF + MLH:C_Z].rearrange("(k p) c -> p k c", p=P)).then_inc(s["gatew_in"], 16)
            sp.dma_start(wg[:, :, MLH:NFD],
                         w_in[0, :, C_DT:C_DT + SSH].rearrange("(k p) c -> p k c", p=P)).then_inc(s["gatew_in"], 16)
            sp.wait_ge(s["par_in"], PAR_DMAS * 16)
            for w, first, passes, base in ((w_in, C_Z, 6, 0), (w_in, 0, 7, 6), (w_out, 0, 4, 13)):
                if base == 6:
                    sp.dma_start(wr[:, :, 0:GRP],
                                 moe_w_group[0].rearrange("(k p) g -> p k g", p=P)).then_inc(s["routerw_in"], 16)
                    for g in range(GRP):
                        sp.dma_start(wr[:, :, GRP + g * EPG:GRP + (g + 1) * EPG],
                                     moe_w_router[0, g].rearrange("(k p) e -> p k e", p=P)).then_inc(s["routerw_in"], 16)
                with sp.Fori(0, passes) as i:
                    for a, landed in enumerate((s["in_a"], s["in_b"])):
                        sp.wait_ge(s["in_ev"], i * 4 + (4 * base + 2 * a + 2))
                        sp.dma_start(wchunk(a), columns(w, i * (2 * CH) + (first + a * CH))).then_inc(landed, 16)

            def expert_weights(n, e):
                for j in range(NSLOT):
                    if j == 4:
                        sp.wait_ge(s["in_ev"], 4 * 17 + 4)
                    sp.wait_ge({3: s["h_ps"], 5: s["y_ps"]}[j] if j in (3, 5) else m_free[j], n + 1)
                    if j < 4:
                        w = (moe_w1, moe_w3)[j % 2]
                        src = w[0, bass.ds(e, 1), (j // 2) * 1024:(j // 2 + 1) * 1024, :].rearrange(
                            "e (k p) f -> p (e k) f", p=P)
                        dst = slot((j + 2) % 6).rearrange("p (k f) -> p k f", f=FE)
                    else:
                        src = moe_w2[0, bass.ds(e, 1), (j - 4) * 256:(j - 3) * 256, :].rearrange(
                            "e (k p) d -> p (e k) d", p=P)
                        dst = slot(j - 4).rearrange("p (k d) -> p k d", d=D)
                    sp.dma_start(dst, src).then_inc(m_in[j], 16)

            with sp.Fori(0, NE) as i:
                expert_weights(i, i)
            sp.wait_ge(s["ov_ready"], 1)
            count = sp.value_load(ov_n[0:1, 0:1], min_val=0, max_val=NOV)
            with sp.If(count > 0):
                with sp.Fori(0, count) as i:
                    e = sp.value_load(ov_e[0:1, bass.ds(i, 1)], min_val=0, max_val=NE - 1)
                    expert_weights(i + NE, e)
            for tb in range(2):
                if tb == 0:
                    sp.wait_ge(s["y_out"], 1)
                rows = yd[(NM + tb * P) * 4:(NM + (tb + 1) * P) * 4, :].rearrange(
                    "(t j h) d -> t j (h d)", j=2, h=2)
                for j in range(2):
                    sp.dma_start(slot(tb)[:, j * D:(j + 1) * D], rows[:, j, :]).then_inc(yt_in[tb][j], 16)
            for tb in range(2):
                sp.wait_ge(s["f_done"], tb + 1)
                sp.dma_start(out[0, tb * P:(tb + 1) * P, :], slot(tb)[:, 0:D]).then_inc(s["out_sem"], 16)
            sp.wait_ge(s["out_sem"], 32)

        @block.gpsimd
        def _(pool):
            V = nc.gpsimd
            step = Steps(pool, s["pool_steps"])
            V.memset(ones[:, :], 1.0)
            step.link(V.memset(ident[:, :], 0.0))
            V.affine_select(out=ident[:, :], in_=ident[:, :], compare_op=ALU.not_equal, fill=1.0, base=0,
                            pattern=[[-1, P]], channel_multiplier=1).then_inc(s["ident_ready"], 1)
            V.memset(mcaus[:, :], 1.0)
            V.memset(mlev[:, :, :], 0.0)
            V.memset(before[:, :], 1.0)
            V.memset(wg[:, :, NFD:IG0], 0.0)
            step.link(V.memset(sel[0:NFD, :, :], 0.0))
            V.affine_select(out=before[:, :], in_=before[:, :], compare_op=ALU.is_gt, fill=0.0, base=0,
                            pattern=[[1, P]], channel_multiplier=-1)
            for c, n in ((0, P), (WS0, P), (WS0 + WS1, TL)):
                V.affine_select(out=mcaus[:, c:c + n], in_=mcaus[:, c:c + n], compare_op=ALU.is_ge, fill=0.0,
                                base=0, pattern=[[1, n]], channel_multiplier=-1)
            V.affine_select(out=sel[0:NFD, :, :], in_=sel[0:NFD, :, :], compare_op=ALU.not_equal, fill=1.0,
                            base=0, pattern=[[-1, NFD], [0, P]], channel_multiplier=1)
            for li, h in enumerate(LV):
                m = mlev[:, li, :].rearrange("p (b r h) -> p b r h", r=2, h=h)[:, :, 1, :]
                step.link(V.memset(m, 1.0))
                step.link(V.affine_select(out=m, in_=m, compare_op=ALU.is_ge, fill=0.0, base=0,
                                          pattern=[[-2 * h, P // (2 * h)], [0, h]], channel_multiplier=1))
                last = V.affine_select(out=m, in_=m, compare_op=ALU.is_ge, fill=0.0, base=h - 1,
                                       pattern=[[2 * h, P // (2 * h)], [0, h]], channel_multiplier=-1)
            last.then_inc(s["consts"], 1)

            pool.wait_ge(s["in_ev"], 4 * 17 + 4)
            V.iota(io_e, pattern=[[1, NE]], base=0, channel_multiplier=0, allow_small_or_imprecise_dtypes=True)
            V.iota(io_s, pattern=[[0, 2], [1, CAP]], base=0, channel_multiplier=0,
                   allow_small_or_imprecise_dtypes=True)
            V.iota(io_t, pattern=[[2 * P, NT], [1, 2]], base=0, channel_multiplier=2,
                   allow_small_or_imprecise_dtypes=True)
            V.iota(io_c, pattern=[[0, NB - 1], [1, NE]], base=0, channel_multiplier=0,
                   allow_small_or_imprecise_dtypes=True)
            step.link(V.memset(half, 0.0))
            step.link(V.memset(half[64:P, :], 1.0))
            V.memset(xs, 0.0).then_inc(s["iotas"], 1)

            last_half, last_row = pool.to_reg(2 * T - 1), pool.to_reg(4 * T - 1)

            def waited():
                pool.sem_inc(s["pool_waited"], 1)

            def gather(m, col, freed=None):
                if freed is not None:
                    pool.wait_ge(s["xT_ps"], freed)
                    waited()
                V.tensor_copy(xcol[:, :], col).then_inc(s["col_x"], 1)
                pool.wait_ge(s["col_x"], m + 1)
                waited()
                V.indirect_dma_start(out=xs, out_offset=None, in_=u2d[:, :],
                                     in_offset=bass.IndirectOffsetOnAxis(ap=xcol[:, 0:1], axis=0),
                                     bounds_check=last_half, oob_is_err=False).then_inc(s["xs_in"], 16)

            def scatter(n, col):
                V.tensor_copy(ycol[:, :], col).then_inc(s["col_y"], 1)
                pool.wait_ge(s["col_y"], n + 1)
                pool.wait_ge(s["y_act"], n + 1)
                pool.wait_ge(s["y_dve"], n + 1)
                waited()
                V.indirect_dma_start(out=yd[:, :],
                                     out_offset=bass.IndirectOffsetOnAxis(ap=ycol[:, 0:1], axis=0),
                                     in_=ysb, in_offset=None,
                                     bounds_check=last_row, oob_is_err=False).then_inc(s["ys_out"], 16)
                pool.wait_ge(s["ys_out"], n * 16 + 16)
                pool.sem_inc(s["y_free"], 1)

            pool.wait_ge(s["u2_out"], NT * 16)
            pool.wait_ge(s["idx_ready"], 1)
            pool.sem_inc(s["y_free"], 1)
            gather(0, idx_x[:, 0:1])
            with pool.Fori(0, NE) as i:
                gather(i + 1, idx_x[:, bass.ds(i + 1, 1)], i + 1)
                scatter(i, idx_y[:, bass.ds(i, 1)])
            pool.wait_ge(s["xs_in"], NE * 16 + 16)
            pool.wait_ge(s["ov_ready"], 1)
            count = pool.value_load(ov_n[0:1, 0:1], min_val=0, max_val=NOV)
            with pool.If(count > 0):
                with pool.Fori(0, count) as i:
                    gather(i + (NE + 1), ov_x[:, bass.ds(i, 1)], i + NE)
                    scatter(i + NE, ov_y[:, bass.ds(i, 1)])
            V.memset(xcol[:, :], 0).then_inc(s["y_out"], 1)

        @block.scalar
        def _(act):
            V = nc.scalar
            step = Steps(act, s["act_steps"])
            act.sem_inc(s["in_ev"], 4)
            act.sem_inc(s["conv_done"], 4)
            par_dmas = [(par_rows[PM:PM + 16, :], norm_mix_w[0].rearrange("(r c) -> r c", c=P)),
                        (par_rows[PF:PF + 16, :], norm_ffn_w[0].rearrange("(r c) -> r c", c=P)),
                        (par_rows[PH_:PH_ + 4, :], hg_norm_w[0].rearrange("(r c) -> r c", c=P)),
                        (par_rows[PL:PL + 4, :], ml_norm_w[0].rearrange("(r c) -> r c", c=P)),
                        (par_rows[PS:PS + 8, :], ssm_norm_w[0].rearrange("(r c) -> r c", c=P)),
                        (par_rows[PW:PW + 64, :], ssm_conv_w[0].rearrange("j (r c) -> (j r) c", c=P)),
                        (par_rows[PB:PB + 16, :], ssm_conv_b[0].rearrange("(r c) -> r c", c=P)),
                        (lb_rows[0:4, :], hg_lb_logits[0].rearrange("(r c) -> r c", c=P)),
                        (dB[:, :], ssm_d[0].partition_broadcast(P)),
                        (brow[:, 0:GRP], moe_b_group[0].partition_broadcast(P)),
                        (brow[:, GRP:GRP + NE], moe_b_router[0].rearrange("g e -> (g e)").partition_broadcast(P))]
            for dst, src in par_dmas:
                act.dma_start(dst, src).then_inc(s["par_in"], 16)
            assert len(par_dmas) == PAR_DMAS

            act.wait_ge(s["params_zeroed"], 1)
            junk = uT[:, 0:8, :].rearrange("p k t -> p (k t)")[:, 0:D]
            for a, (_, n) in enumerate(TT):
                act.wait_ge(X_IN[a][0], 16 * X_IN[a][1])
                if a:
                    act.wait_ge(s["act_steps"], step.n)
                step.link(V.activation(junk[0:n, :], xin[0:n, a, :], ACT.Square, accum_out=ss3[0:n, a:a + 1]))
            step.link(V.activation(rs3[:, :], ss3[:, :], ACT.Ln, scale=1.0 / D, bias=epsc[:, 0:1]))
            V.activation(rs3[:, :], rs3[:, :], ACT.Exp, scale=-0.5).then_inc(s["rms_ready"], 1)
            for dst, src in ((gcols[0:MLH, 0:1], ml_b_f), (gcols[MLH:NFD, 0:1], ssm_dt_bias),
                             (gcols[MLH:NFD, 1:2], ssm_a_log), (gcols[0:MLH, 2:3], ml_b_i)):
                act.dma_start(dst, src[0].rearrange("(r c) -> r c", c=1)).then_inc(s["gate_cols_in"], 16)
            act.wait_ge(s["lb_diff"], 1)
            V.activation(lb4[:, 1, :], lb4[:, 0, :], ACT.Exp).then_inc(s["lb_exp"], 1)
            act.wait_ge(s["gate_cols_in"], 64)
            V.activation(gcols[:, 1:2], gcols[:, 1:2], ACT.Exp).then_inc(s["alog_exp"], 1)

            act.wait_ge(s["gf_ready"], 1)
            act.wait_ge(s["gcols_ready"], 1)
            V.activation(gL[:, :], pb[5][IG0:IG0 + MLH, 0:T], ACT.Tanh, scale=1.0 / 15, bias=gcols[0:MLH, 2:3]).then_inc(
                s["li_ready"], 1)
            act.wait_ge(s["fd_x"], 1)
            V.activation(gX[0:MLH, :], gX[0:MLH, :], ACT.Tanh, scale=1.0 / 15).then_inc(s["fd_tanh"], 1)
            act.wait_ge(s["fd_x"], 2)
            step.link(V.activation(gQ[:, :], gX[:, :], ACT.Abs))
            V.activation(gQ[:, :], gQ[:, :], ACT.Exp, scale=-1.0).then_inc(s["fd_e"], 1)
            act.wait_ge(s["em_t"], 1)
            V.activation(gZ[0:MLH, :], gZ[0:MLH, :], ACT.Exp, scale=-1.0).then_inc(s["em_exp"], 1)

            def tiles_out(i, base, func):
                for b in range(4):
                    act.wait_ge(s["in_tile"], i * 4 + (4 * base + b + 1))
                    V.activation(proj[:, bass.ds(i * 4 + (4 * base + b), 1), :].rearrange("p a t -> p (a t)"),
                                 pb[b][:, 0:T], func).then_inc(s["in_ev"], 1)

            def conv_out(i, b):
                act.wait_ge(s["conv_acc"], i * 4 + (b + 1))
                V.activation(proj[:, bass.ds(i * 4 + (X0 + b), 1), :].rearrange("p a t -> p (a t)"),
                             conv[b], ACT.Silu).then_inc(s["conv_done"], 1)

            with act.Fori(0, 2) as i:
                tiles_out(i, 0, ACT.Silu)
            tiles_out(0, 2, ACT.Copy)
            with act.Fori(0, 3) as i:
                tiles_out(i, 3, ACT.Copy)
                for b in range(4):
                    conv_out(i, b)

            def tile_out(g, func=ACT.Copy):
                act.wait_ge(s["in_tile"], g + 1)
                V.activation(proj[:, g, :], pb[g % 4][:, 0:T], func).then_inc(s["in_ev"], 1)

            for a, (_, n) in enumerate(TT):
                for part in range(2):
                    act.wait_ge(s["xv_T"], 2 * a + part + 1)
                    V.activation(xv[0:n, a, part * 512:(part + 1) * 512], pb[4 + (2 * a + part) % 4][0:n, :],
                                 ACT.Copy).then_inc(s["xv_ev"], 1)
            for b in range(4):
                conv_out(3, b)

            for u in range(16):
                for e in HEADS_AT[u]:
                    act.wait_ge(s["e_ready"], e + 1)
                    V.activation(E2[:, e % 2, 0:WS0 + WS1], E2[:, e % 2, 0:WS0 + WS1], ACT.Exp)
                    V.activation(E2[0:TL, e % 2, WS0 + WS1:PW_], E2[0:TL, e % 2, WS0 + WS1:PW_],
                                 ACT.Exp).then_inc(s["e_exp"], 1)
                tile_out(HQ + u)

            norm_no = [0]

            def squares(made, count, src, sq, groups, tiles):
                act.wait_ge(made, count)
                V.activation(sq[:, 0:groups * tiles, :], src, ACT.Square).then_inc(s["sq_ready"], 1)

            def inverse_rms(groups, tiles):
                for g in range(groups):
                    act.wait_ge(s["sum_ready"], 4 * norm_no[0] + g + 1)
                    last = V.activation(rs4[:, g, :], pb[4 + g][:, 0:T], ACT.Ln, scale=1.0 / (P * tiles),
                                        bias=epsc[:, 0:1])
                step.link(last)
                V.activation(rs4[:, :, :], rs4[:, :, :], ACT.Exp, scale=-0.5).then_inc(s["rs_ready"], 1)
                norm_no[0] += 1

            squares(s["ssm_gated"], 1, proj[:, Z0:Z0 + 8, :], sq8, 4, 2)
            tile_out(MQ)
            tile_out(MQ + 1)
            inverse_rms(4, 2)

            act.wait_ge(s["in_ev"], HG_ + 4 + 4)
            V.activation(W[0][:, :, :], proj[:, HF:HF + 4, :], ACT.Sigmoid).then_inc(s["hsig"], 1)
            V.activation(proj[:, HF:HF + 4, :], proj[:, HF:HF + 4, :], ACT.Sigmoid, scale=-1.0).then_inc(s["hsig"], 1)
            V.activation(proj[:, HG_:HG_ + 4, :], proj[:, HG_:HG_ + 4, :], ACT.Silu).then_inc(s["hg_gate"], 1)
            tile_out(MQ + 2)
            act.wait_ge(s["hlin"], 1)
            V.activation(W[0][:, :, :], W[0][:, :, :], ACT.Ln).then_inc(s["hln"], 1)

            def v_out(c):
                a, n = c % 3, TT[c % 3][1]
                act.wait_ge(s["hv_T"], c + 1)
                V.activation((hv, mv)[c // 3][0:n, a, :], pb[7][0:n, :], ACT.Copy).then_inc(s["hv_ev"], 1)

            for c in range(3):
                v_out(c)
            for u in range(5):
                tile_out(MQ + 3 + u)
                for l in LEVELS_AT[u]:
                    if l >= 0:
                        act.wait_ge(s["lv_d"], l + 1)
                        n = LWID[l]
                        V.activation(W[l % 2][:, :, 0:n], W[l % 2][:, :, 0:n], ACT.Exp).then_inc(s["lv_e"], 1)
            for c in range(3, 6):
                v_out(c)
            for h in range(MLH):
                tile_out(MO + h)
                act.wait_ge(s["ml_e"], h + 1)
                V.activation(E2[:, h % 2, 0:WS0 + WS1], E2[:, h % 2, 0:WS0 + WS1], ACT.Exp, scale=-1.0)
                V.activation(E2[0:TL, h % 2, WS0 + WS1:PW_], E2[0:TL, h % 2, WS0 + WS1:PW_], ACT.Exp,
                             scale=-1.0).then_inc(s["ml_exp"], 1)
                act.wait_ge(s["ml_o"], h + 1)
                V.activation(mden[:, :], pb[7][:, 0:T], ACT.Abs).then_inc(s["ml_abs"], 1)
            squares(s["ml_h"], MLH, proj[:, HQ:HQ + 4, :], sqH, 4, 1)
            act.wait_ge(s["in_ev"], 4 * 13 + 4)
            V.activation(proj[:, MO:MO + 4, :], proj[:, MO:MO + 4, :], ACT.Sigmoid).then_inc(s["mo_gate"], 1)
            inverse_rms(4, 1)
            squares(s["hg_done"], 1, W[1][:, :, :], sqH, 4, 1)
            inverse_rms(4, 1)

            for k in range(KD):
                act.wait_ge(s["in_ev"], 4 * 13 + 4 + k + 1)
                if k >= 8:
                    act.wait_ge(s["sq_acc"], k - 6)
                V.activation(sqk[:, k % 8, :], hT[:, k, :], ACT.Square).then_inc(s["sq2"], 1)
                V.activation(uT[:, k, :], hT[:, k, :], ACT.Copy, scale=par[:, PF + k:PF + k + 1]).then_inc(
                    s["u2T_ready"], 1)
            act.wait_ge(s["sum2"], 1)
            V.activation(rs3[:, 0:NT - 1], pb[6][:, 0:NT - 1], ACT.Ln, scale=1.0 / D, bias=epsc[:, 0:1])
            step.link(V.activation(rs3[0:TL, NT - 1:NT], pb[6][0:TL, NT - 1:NT], ACT.Ln, scale=1.0 / D,
                                   bias=epsc[0:TL, 0:1]))
            V.activation(rs3[:, :], rs3[:, :], ACT.Exp, scale=-0.5).then_inc(s["rs2"], 1)
            act.wait_ge(s["rs2"], 1)
            for a, (_, n) in enumerate(TT):
                for q in range(4):
                    act.wait_ge(s["t_ps"], 4 * a + q + 1)
                    V.activation(u2[0:n, a, q * 512:(q + 1) * 512], pb[q][0:n, :], ACT.Copy,
                                 scale=rs3[0:n, a:a + 1]).then_inc(s["t_ev"], 1)
                act.wait_ge(s["t_ev"], 4 * a + 4)
                t0 = TT[a][0]
                act.dma_start(u2d[2 * t0:2 * (t0 + n), :].rearrange("(t h) d -> t (h d)", h=2),
                              u2[0:n, a, :]).then_inc(s["u2_out"], 16)
            act.wait_ge(s["gmax"], 1)
            V.activation(rt_ex, rt_ex, ACT.Exp).then_inc(s["gmax_e"], 1)
            act.wait_ge(s["u2_out"], NT * 16)
            for tb in range(2):
                for q in range(4):
                    act.wait_ge(s["h2_ps"], 4 * tb + q + 1)
                    V.activation(h2[:, tb, q * 512:(q + 1) * 512], pb[4 * tb + q][:, :], ACT.Copy).then_inc(
                        s["h2_ev"], 1)
            act.dma_start(fw, final_norm_w.partition_broadcast(P)).then_inc(s["fw_in"], 16)

            def expert(n, wcol):
                act.wait_ge(s["xT_ps"], n + 1)
                V.activation(xsT[:, 0:4, :, :].rearrange("p c h s -> p (c h s)"), pb[0][:, :],
                             ACT.Copy).then_inc(s["xT_ev"], 1)
                act.wait_ge(s["h_ps"], n + 2)
                V.activation(hs, pb[2][:, :], ACT.Copy).then_inc(s["h_ev"], 1)
                act.wait_ge(s["hT_ps"], n + 1)
                V.activation(ssb, hid_ps[:, :, 0:CAP], ACT.Silu).then_inc(s["silu_ev"], 1)
                act.wait_ge(s["y_ps"], n + 2)
                act.wait_ge(s["y_free"], n + 1)
                V.activation(ysb[:, 0:512], pb[4][:, :], ACT.Copy, scale=wcol).then_inc(s["y_act"], 1)

            with act.Fori(0, NE) as i:
                expert(i, idx_base[:, 2, bass.ds(i, 1)])
            act.wait_ge(s["ov_ready"], 1)
            count = act.value_load(ov_n[0:1, 0:1], min_val=0, max_val=NOV)
            with act.If(count > 0):
                with act.Fori(0, count) as i:
                    expert(i + NE, ov_w[:, bass.ds(i, 1)])
            for tb in range(2):
                act.wait_ge(s["f_sum"], tb + 1)
                step.link(V.activation(slot(tb)[:, D:2 * D], h2[:, tb, :], ACT.Square,
                                       accum_out=fss[:, tb:tb + 1]))
                step.link(V.activation(frs[:, tb:tb + 1], fss[:, tb:tb + 1], ACT.Ln, scale=1.0 / D,
                                       bias=epsc[:, 0:1]))
                V.activation(frs[:, tb:tb + 1], frs[:, tb:tb + 1], ACT.Exp, scale=-0.5).then_inc(s["f_rs"], 1)

        @block.vector
        def _(dve):
            V = nc.vector
            step = Steps(dve, s["dve_steps"])
            V.memset(epsc[:, :], EPS)
            V.memset(ss3[:, :], 1.0)
            V.memset(gcols[:, :], 0.0).then_inc(s["params_zeroed"], 1)
            for k in range(KD):
                dve.wait_ge(s["x_T"], k + 1)
                V.tensor_copy(hT[:, k, :], pb[k % 4][:, 0:T]).then_inc(s["x_ev"], 1)
            dve.wait_ge(s["par_T"], 1)
            V.tensor_copy(par[:, :], pb[7][:, 0:P + 4]).then_inc(s["par_ev"], 1)
            dve.wait_ge(s["par_ev"], 1)
            V.tensor_tensor(lb4[:, 0, :], par[:, P:P + 4], par[:, P:P + 4], ALU.subtract).then_inc(s["lb_diff"], 1)
            dve.wait_ge(s["ident_ready"], 1)
            dve.wait_ge(s["rms_ready"], 1)
            for a, (_, n) in enumerate(TT):
                last = V.tensor_scalar(dg[0:n, a, 0:n], ident[0:n, 0:n], rs3[0:n, a:a + 1], None, ALU.mult)
            last.then_inc(s["diag_ready"], 1)
            dve.wait_ge(s["R_ready"], 1)
            step.link(V.tensor_copy(Rb[:, :], pb[6][:, 0:T]))
            for k in range(KD):
                dve.wait_ge(s["x_ev"], k + 1)
                V.scalar_tensor_tensor(uT[:, k, :], hT[:, k, :], par[:, PM + k:PM + k + 1], Rb[:, :],
                                       ALU.mult, ALU.mult).then_inc(s["uT_ready"], 1)
            dve.wait_ge(s["consts"], 1)
            dve.wait_ge(s["lb_exp"], 1)
            step.link(V.reciprocal(lb4[:, 2, :], lb4[:, 1, :]))
            step.link(V.tensor_tensor(lb4[:, 0, :], lb4[:, 1, :], lb4[:, 2, :], ALU.mult))
            step.link(V.tensor_tensor(lb4[:, 3, :], lb4[:, 0, :], lb4[:, 0, :], ALU.subtract))
            step.link(V.tensor_scalar(lb4[:, 1, :], lb4[:, 3, :], 1e-30, None, ALU.max))
            V.tensor_scalar(lb4[:, 0, :], lb4[:, 3, :], -1.0, 1.0, ALU.mult, ALU.add)
            step.link(V.tensor_tensor(lb4[:, 2, :], lb4[:, 3, :], lb4[:, 1, :], ALU.subtract))
            V.tensor_copy(dcol[0:64, :], dB[0:64, :].rearrange("p (c r) -> p c r", r=2)[:, :, 0])
            step.link(V.tensor_copy(dcol[64:P, :], dB[64:P, :].rearrange("p (c r) -> p c r", r=2)[:, :, 1]))
            dve.wait_ge(s["alog_exp"], 1)
            V.tensor_scalar(gcols[:, 1:2], gcols[:, 1:2], -1.0, None, ALU.mult)
            V.tensor_scalar(gcols[:, 2:3], gcols[:, 2:3], 1.0 / 15, None, ALU.mult).then_inc(s["gcols_ready"], 1)

            dve.wait_ge(s["gf_ready"], 1)
            dve.wait_ge(s["gcols_ready"], 1)
            V.tensor_scalar(gX[:, :], pb[5][0:NFD, 0:T], gcols[:, 0:1], None, ALU.add).then_inc(s["fd_x"], 1)
            dve.wait_ge(s["fd_tanh"], 1)
            V.tensor_scalar(gX[0:MLH, :], gX[0:MLH, :], -15.0, None, ALU.mult).then_inc(s["fd_x"], 1)
            dve.wait_ge(s["fd_e"], 1)
            step.link(V.tensor_scalar(gA[:, :], gQ[:, :], 2.0, None, ALU.add))
            step.link(V.reciprocal(gZ[:, :], gA[:, :]))
            step.link(V.tensor_tensor(gA[:, :], gQ[:, :], gZ[:, :], ALU.mult))
            step.link(V.tensor_tensor(gZ[:, :], gA[:, :], gA[:, :], ALU.mult))
            step.link(V.tensor_scalar(gQ[:, :], gZ[:, :], 1.0 / 15, None, ALU.mult))
            for c in (13, 11, 9, 7, 5, 3):
                step.link(V.scalar_tensor_tensor(gQ[:, :], gQ[:, :], 1.0 / c, gZ[:, :], ALU.add, ALU.mult))
            step.link(V.scalar_tensor_tensor(gQ[:, :], gQ[:, :], 1.0, gA[:, :], ALU.add, ALU.mult))
            step.link(V.tensor_scalar(gX[:, :], gX[:, :], 0.0, None, ALU.max))
            step.link(V.scalar_tensor_tensor(gA[:, :], gQ[:, :], 2.0, gX[:, :], ALU.mult, ALU.add))
            step.link(V.tensor_scalar(gQ[:, :], gA[:, :], gcols[:, 1:2], None, ALU.mult))
            step.link(V.tensor_tensor_scan(gX[:, :], ones[0:NFD, :], gQ[:, :], 0.0, ALU.mult, ALU.add))
            dve.wait_ge(s["li_ready"], 1)
            step.link(V.scalar_tensor_tensor(gL[:, :], gL[:, :], 15.0, gX[0:MLH, :], ALU.mult, ALU.subtract))
            step.link(V.tensor_tensor_scan(gG[:, :], gL[:, :], gL[:, :], 0.0, ALU.max, ALU.max))
            V.tensor_tensor(gZ[0:MLH, :], gG[:, :], gX[0:MLH, :], ALU.add).then_inc(s["em_t"], 1)
            dve.wait_ge(s["em_exp"], 1)
            V.tensor_scalar(gZ[0:MLH, :], gZ[0:MLH, :], 1e37, None, ALU.min).then_inc(s["g_rows"], 1)
            dve.wait_ge(s["g_col"], 1)
            for a, (_, n) in enumerate(TT):
                last = V.tensor_copy(colc[0:n, a, :], pb[6][0:n, 64 * a:64 * a + 2 * NFD + MLH])
            last.then_inc(s["g_colev"], 1)
            dve.wait_ge(s["g_colev"], 1)

            with dve.Fori(0, 4) as i:
                step.enter(i, 12)
                for b in range(4):
                    dve.wait_ge(s["in_ev"], i * 4 + (X0 + b + 1 + 4))
                    dve.wait_ge(s["conv_done"], i * 4 + (b + 1))
                    raw = proj[:, bass.ds(i * 4 + (X0 + b), 1), :].rearrange("p a t -> p (a t)")

                    def tap(j):
                        return par[:, bass.ds(i * 4 + (PW + 16 * j + b), 1)]

                    step.link(V.tensor_scalar(conv[b], raw, tap(3), par[:, bass.ds(i * 4 + (PB + b), 1)],
                                              ALU.mult, ALU.add))
                    for j in (2, 1, 0):
                        d = CONVW - 1 - j
                        shifted = proj[:, bass.ds(i * 4 + (X0 + b), 1), 0:T - d].rearrange("p a t -> p (a t)")
                        last = V.scalar_tensor_tensor(conv[b][:, d:T], shifted, tap(j), conv[b][:, d:T],
                                                      ALU.mult, ALU.add)
                        if j:
                            step.link(last)
                    last.then_inc(s["conv_acc"], 1)
                step.leave(4)

            for g in range(SSG):
                dve.wait_ge(s["cb_ready"], g + 1)
                V.tensor_tensor(CB[:, g, 0:WS0 + WS1], pb[4 + g][:, 0:WS0 + WS1], mcaus[:, 0:WS0 + WS1], ALU.mult)
                last = V.tensor_tensor(CB[0:TL, g, WS0 + WS1:PW_], pb[4 + g][0:TL, WS0 + WS1:PW_],
                                       mcaus[0:TL, WS0 + WS1:PW_], ALU.mult)
            last.then_inc(s["cb_ev"], 1)
            dve.wait_ge(s["cb_ev"], 1)

            def ssm_decay(e):
                dve.wait_ge(s["bc_ready"], e + 1)
                for c, a, t, n in SC:
                    r = TT[a][1]
                    last = V.tensor_scalar(E2[0:r, e % 2, c:c + n], pb[4 + e % 2][0:r, t:t + n],
                                           colc[0:r, a, MLH + e:MLH + e + 1], 0.0, ALU.subtract, ALU.min)
                last.then_inc(s["e_ready"], 1)

            def ssm_scores(e):
                dve.wait_ge(s["e_exp"], e + 1)
                if e >= 2:
                    dve.wait_ge(s["y_ready"], e - 1)
                for c, a, t, n in SC:
                    r = TT[a][1]
                    last = V.scalar_tensor_tensor(P2[0:r, e % 2, c:c + n], E2[0:r, e % 2, c:c + n],
                                                  colc[0:r, a, NFD + MLH + e:NFD + MLH + e + 1],
                                                  CB[0:r, e // 4, c:c + n], ALU.mult, ALU.mult)
                last.then_inc(s["pt_ready"], 1)

            def ssm_out(c):
                dve.wait_ge(s["y_ready"], 2 * c + 2)
                V.scalar_tensor_tensor(proj[:, X0 + c, :], proj[:, X0 + c, :], dcol[:, c:c + 1],
                                       pb[6 + c % 2][:, 0:T], ALU.mult, ALU.add).then_inc(s["y_ev"], 1)
                dve.wait_ge(s["y_ev"], c + 1)
                return V.tensor_tensor(proj[:, Z0 + c, :], proj[:, Z0 + c, :], proj[:, X0 + c, :], ALU.mult)

            for e in range(SSH + 1):
                if e < SSH:
                    ssm_decay(e)
                if e >= 1:
                    ssm_scores(e - 1)
                if e >= 4 and e % 2 == 0:
                    ssm_out(e // 2 - 2)
            ssm_out(SSH // 2 - 1).then_inc(s["ssm_gated"], 1)
            norm_no = [0]

            def group_norm(src, dst, gate, groups, tiles, pcol):
                dve.wait_ge(s["rs_ready"], norm_no[0] + 1)
                for c in range(groups * tiles):
                    last = V.scalar_tensor_tensor(dst(c), src(c), par[:, pcol + c:pcol + c + 1],
                                                  rs4[:, c // tiles, :], ALU.mult, ALU.mult)
                if gate is not None:
                    step.link(last)
                    for c in range(groups * tiles):
                        last = V.tensor_tensor(gate(c), gate(c), dst(c), ALU.mult)
                norm_no[0] += 1
                return last

            group_norm(lambda c: proj[:, Z0 + c, :], lambda c: proj[:, Z0 + c, :], None, 4, 2, PS)

            dve.wait_ge(s["in_ev"], HV + 4)
            dve.wait_ge(s["hsig"], 2)
            for h in range(HGH):
                V.tensor_scalar(W[0][:, h, :], W[0][:, h, :], lb4[:, 0, h:h + 1], lb4[:, 1, h:h + 1],
                                ALU.mult, ALU.add)
                V.tensor_scalar(proj[:, HF + h, :], proj[:, HF + h, :], lb4[:, 0, h:h + 1],
                                lb4[:, 2, h:h + 1], ALU.mult, ALU.add)
            V.tensor_scalar(proj[:, HQ:HQ + 4, :], proj[:, HQ:HQ + 4, :], float(P) ** -0.5, None,
                            ALU.mult).then_inc(s["hlin"], 1)
            V.memset(PHs[:, :, :], 0.0)
            dve.wait_ge(s["hln"], 1)
            for h in range(HGH):
                last = V.tensor_tensor_scan(cumT[:, h, :], ones[:, :], W[0][:, h, :], 0.0, ALU.mult, ALU.add)
            step.link(last)

            def halves(t, l):
                h = LH[l]
                if l == NLEV - 1:
                    return t[:, :, 0:2 * P], t[:, :, 2 * P:T]
                if h <= 8:
                    v = t.rearrange("p a (b r h) -> p (a b) r h", r=2, h=h)
                    return v[:, :, 0, :], v[:, :, 1, :]
                v = t[:, :, 0:2 * P].rearrange("p a (b r h) -> p a b r h", r=2, h=h)
                return v[:, :, :, 0, :], v[:, :, :, 1, :]

            def level_diff(l):
                if l >= 2:
                    dve.wait_ge(s["lv_ps"], l - 1)
                h = LH[l]
                cl, cr = halves(cumT, l)
                wl, wr_ = halves(W[l % 2], l)
                ref = cl[:, :, h - 1:h] if len(cl.shape) == 3 else cl[:, :, :, h - 1:h]
                V.tensor_tensor(wl, ref.to_broadcast(list(cl.shape)), cl, ALU.subtract)
                V.tensor_tensor(wr_, cr, ref.to_broadcast(list(cr.shape)), ALU.subtract).then_inc(s["lv_d"], 1)

            def level_scale(l):
                dve.wait_ge(s["lv_e"], l + 1)
                wl, wr_ = halves(W[l % 2], l)
                kl, _ = halves(proj[:, HF:HF + 4, :], l)
                _, qr = halves(proj[:, HQ:HQ + 4, :], l)
                V.tensor_tensor(wl, wl, kl, ALU.mult)
                V.tensor_tensor(wr_, wr_, qr, ALU.mult).then_inc(s["lv_w"], 1)

            def level_store(l):
                if l < 0:
                    dve.wait_ge(s["lvd_ps"], 1)
                else:
                    dve.wait_ge(s["lv_ps"], l + 1)
                    dve.wait_ge(s["lv_ev"], l + 1)
                b = 4
                if l < 7:
                    m = ident[:, :] if l < 0 else mlev[:, l, :]
                    m = m.bitcast(u32)
                    for a in range(2):
                        c = (0, WS0)[a]
                        last = V.copy_predicated(
                            PHs[:, :, c:c + P], m.unsqueeze(1).to_broadcast([P, 4, P]),
                            pb[b + a][:, :].rearrange("p (h t) -> p h t", h=4))
                    if l < 0 or LH[l] <= 8:
                        last = V.copy_predicated(
                            PHs[0:TL, :, WS0 + WS1:PW_], m[0:TL, 0:TL].unsqueeze(1).to_broadcast([TL, 4, TL]),
                            pb[b + 2][0:TL, 0:4 * TL].rearrange("p (h t) -> p h t", h=4))
                elif l == 7:
                    last = V.tensor_copy(PHs[:, :, P:2 * P], pb[b][:, :].rearrange("p (h t) -> p h t", h=4))
                else:
                    v = pb[b][:, 0:8 * TL].rearrange("p (a h t) -> p a h t", a=2, h=4)
                    V.tensor_copy(PHs[:, :, 2 * P:T], v[:, 0, :, :])
                    last = V.tensor_copy(PHs[:, :, T + P:T + WS1], v[:, 1, :, :])
                last.then_inc(s["lv_ev"], 1)

            level_diff(0)
            level_store(-1)
            for l in range(NLEV):
                if l + 1 < NLEV:
                    level_diff(l + 1)
                level_scale(l)
                if l >= 1:
                    level_store(l - 1)
            level_store(NLEV - 1)
            for h in range(HGH):
                dve.wait_ge(s["ho_ps"], h + 1)
                last = V.tensor_copy(proj[:, HQ + h, :], pb[4 + h % 2][:, 0:T])
                last.then_inc(s["ho_ev"], 1)

            for h in range(MLH):
                dve.wait_ge(s["ml_ps"], h + 1)
                for c, a, t, n in SC:
                    r = TT[a][1]
                    last = V.tensor_scalar(E2[0:r, h % 2, c:c + n], pb[5][0:r, t:t + n],
                                           colc[0:r, a, 2 * NFD + h:2 * NFD + h + 1], 0.0, ALU.subtract, ALU.max)
                last.then_inc(s["ml_e"], 1)
                dve.wait_ge(s["ml_exp"], h + 1)
                for lo, hi, r in ((0, WS0 + WS1, P), (WS0 + WS1, PW_, TL)):
                    last = V.scalar_tensor_tensor(P2[0:r, h % 2, lo:hi], E2[0:r, h % 2, lo:hi],
                                                  float(MLQ) ** -0.5, pb[4][0:r, lo:hi], ALU.mult, ALU.mult)
                step.link(last)
                V.tensor_tensor(P2[:, h % 2, 0:WS0 + WS1], P2[:, h % 2, 0:WS0 + WS1],
                                mcaus[:, 0:WS0 + WS1], ALU.mult)
                V.tensor_tensor(P2[0:TL, h % 2, WS0 + WS1:PW_], P2[0:TL, h % 2, WS0 + WS1:PW_],
                                mcaus[0:TL, WS0 + WS1:PW_], ALU.mult).then_inc(s["ml_pt"], 1)
                dve.wait_ge(s["ml_o"], h + 1)
                dve.wait_ge(s["ml_abs"], h + 1)
                step.link(V.tensor_tensor(mden[:, :], mden[:, :], pb[5][:, 0:T], ALU.max))
                step.link(V.reciprocal(mden[:, :], mden[:, :]))
                last = V.tensor_tensor(W[1][:, h, :], mden[:, :], pb[6][:, 0:T], ALU.mult)
                last.then_inc(s["ml_h"], 1)
            dve.wait_ge(s["hg_gate"], 1)
            dve.wait_ge(s["mo_gate"], 1)
            group_norm(lambda c: proj[:, HQ + c, :], lambda c: proj[:, HQ + c, :],
                       lambda c: proj[:, HG_ + c, :], 4, 1, PH_).then_inc(s["hg_done"], 1)
            group_norm(lambda c: W[1][:, c, :], lambda c: W[1][:, c, :],
                       lambda c: proj[:, MO + c, :], 4, 1, PL).then_inc(s["norm_done"], 1)

            V.memset(sqa, 0.0).then_inc(s["sq_acc"], 1)
            with dve.Fori(0, 4) as i:
                for b in range(4):
                    dve.wait_ge(s["in_tile"], i * 4 + (4 * 13 + b + 1))
                    v = hT[:, bass.ds(i * 4 + b, 1), :].rearrange("p a t -> p (a t)")
                    V.tensor_tensor(v, v, pb[b][:, 0:T], ALU.add).then_inc(s["in_ev"], 1)
                    dve.wait_ge(s["sq2"], i * 4 + (b + 1))
                    dve.wait_ge(s["sq_acc"], i * 4 + (b + 1))
                    q = sqk[:, bass.ds((i * 4) % 8 + b, 1), :].rearrange("p a t -> p (a t)")
                    V.tensor_tensor(sqa, sqa, q, ALU.add).then_inc(s["sq_acc"], 1)
            dve.wait_ge(s["lg_ready"], 1)
            V.tensor_copy(lgT[0:LG, :], pb[4][0:LG, 0:T]).then_inc(s["lg_ev"], 1)
            routing(dve, V, step)

            def expert(n, wcol):
                dve.wait_ge(s["xT_ps"], n + 1)
                V.tensor_copy(xsT[:, 4:8, :, :].rearrange("p c h s -> p (c h s)"), pb[1][:, :]).then_inc(
                    s["xT_ev2"], 1)
                dve.wait_ge(s["silu_ev"], n + 1)
                V.tensor_tensor(hTb, ssb, hid_ps[:, :, CAP:2 * CAP], ALU.mult).then_inc(s["hT_ready"], 1)
                dve.wait_ge(s["y_ps"], n + 2)
                dve.wait_ge(s["y_free"], n + 1)
                V.tensor_scalar(ysb[:, 512:1024], pb[5][:, :], wcol, None, ALU.mult).then_inc(s["y_dve"], 1)

            for n in range(AHEAD):
                expert(n, idx_base[:, 2, n:n + 1])
                further_passes(V, step, n)
            with dve.Fori(AHEAD, NE) as i:
                expert(i, idx_base[:, 2, bass.ds(i, 1)])
            dve.wait_ge(s["ov_ready"], 1)
            count = dve.value_load(ov_n[0:1, 0:1], min_val=0, max_val=NOV)
            with dve.If(count > 0):
                with dve.Fori(0, count) as i:
                    expert(i + NE, ov_w[:, bass.ds(i, 1)])

            dve.wait_ge(s["h2_ev"], 8)
            for tb in range(2):
                dve.wait_ge(yt_in[tb][0], 16)
                y = slot(tb).rearrange("p (j d) -> p j d", j=2)
                step.link(V.tensor_tensor(h2[:, tb, :], h2[:, tb, :], y[:, 0, :], ALU.add))
                dve.wait_ge(yt_in[tb][1], 16)
                V.tensor_tensor(h2[:, tb, :], h2[:, tb, :], y[:, 1, :], ALU.add).then_inc(s["f_sum"], 1)
            dve.wait_ge(s["fw_in"], 16)
            for tb in range(2):
                dve.wait_ge(s["f_rs"], tb + 1)
                V.scalar_tensor_tensor(slot(tb)[:, 0:D], h2[:, tb, :], frs[:, tb:tb + 1], fw,
                                       ALU.mult, ALU.mult).then_inc(s["f_done"], 1)

        @block.tensor
        def _(pe):
            V = nc.tensor

            def product(outs, pairs, start=True, stop=True):
                n = len(pairs)
                for j, (a, b) in enumerate(pairs):
                    last = V.matmul(outs, a, b, start=start and j == 0, stop=stop and j == n - 1)
                return last

            pe.wait_ge(s["ident_ready"], 1)
            for landed, dmas in X_IN:
                pe.wait_ge(landed, 16 * dmas)
            for k in range(KD):
                if k >= 4:
                    pe.wait_ge(s["x_ev"], k - 3)
                for a, (t, n) in enumerate(TT):
                    last = V.transpose(pb[k % 4][:, t:t + n], xin[0:n, a, k * P:(k + 1) * P], ident[0:n, 0:n])
                last.then_inc(s["x_T"], 1)
            pe.wait_ge(s["par_in"], PAR_DMAS * 16)
            V.transpose(pb[7][:, 0:P], par_rows[:, :], ident[:, :])
            V.transpose(pb[7][:, P:P + 4], lb_rows[0:4, :], ident[0:4, 0:4]).then_inc(s["par_T"], 1)
            pe.wait_ge(s["diag_ready"], 1)
            for a, (t, n) in enumerate(TT):
                last = V.matmul(pb[6][:, t:t + n], ones[0:n, 0:P], dg[0:n, a, 0:n], start=True, stop=True)
            last.then_inc(s["R_ready"], 1)

            pe.wait_ge(s["consts"], 1)
            pe.wait_ge(s["gatew_in"], 48)
            for k in range(KD):
                pe.wait_ge(s["uT_ready"], k + 1)
                last = V.matmul(pb[5][0:IG0 + MLH, 0:T], wg[:, k, :], uT[:, k, :], start=k == 0, stop=k == KD - 1)
            last.then_inc(s["gf_ready"], 1)

            def project(passes, base, rhs):
                with pe.Fori(0, passes) as i:
                    for a, landed in enumerate((s["in_a"], s["in_b"])):
                        pe.wait_ge(landed, i * 16 + (base + 1) * 16)
                        for b in range(2):
                            pe.wait_ge(s["in_ev"], i * 4 + (4 * base + 2 * a + b + 1))
                            product(pb[2 * a + b][:, 0:T],
                                    [(wchunk(a)[:, k, b * P:(b + 1) * P], rhs(k)) for k in range(KD)]).then_inc(
                                        s["in_tile"], 1)

            def uT_k(k):
                return uT[:, k, :]

            def tile(g):
                if g % 2 == 0:
                    pe.wait_ge((s["in_a"], s["in_b"])[g // 2 % 2], 16 * (g // 4 + 1))
                pe.wait_ge(s["in_ev"], g + 1)
                product(pb[g % 4][:, 0:T], [(wchunk(g // 2 % 2)[:, k, g % 2 * P:(g % 2 + 1) * P], uT[:, k, :])
                                            for k in range(KD)]).then_inc(s["in_tile"], 1)

            project(2, 0, uT_k)
            pe.wait_ge(s["g_rows"], 1)
            for a, (t, n) in enumerate(TT):
                V.transpose(pb[6][0:n, 64 * a:64 * a + NFD], gX[:, t:t + n], ident[0:NFD, 0:NFD])
                V.transpose(pb[6][0:n, 64 * a + NFD:64 * a + 2 * NFD], gA[:, t:t + n], ident[0:NFD, 0:NFD])
                last = V.transpose(pb[6][0:n, 64 * a + 2 * NFD:64 * a + 2 * NFD + MLH], gL[:, t:t + n],
                                   ident[0:MLH, 0:MLH])
            last.then_inc(s["g_col"], 1)
            project(4, 2, uT_k)

            def by_token(dst_bank, tile0, tiles, a):
                t, n = TT[a]
                for j in range(tiles):
                    last = V.transpose(dst_bank[0:n, j * P:(j + 1) * P], proj[:, tile0 + j, t:t + n], ident[:, :])
                return last

            def row(bank, r, rows, src):
                return V.matmul(bank[:, 0:T], sel[0:rows, r, :], src[0:rows, :], start=True, stop=True)

            def causal(out_, v, scores):
                for j, (c, a, t, n) in enumerate(SC):
                    r = TT[a][1]
                    last = V.matmul(out_[:, t:t + n], v(a, r), scores(r, c, n), start=j == 0, stop=j == NT - 1)
                return last

            pe.wait_ge(s["conv_done"], 8 + 4)
            pe.wait_ge(s["g_colev"], 1)
            for a in range(NT):
                for part in range(2):
                    m = 2 * a + part
                    if m >= 4:
                        pe.wait_ge(s["xv_ev"], m - 3)
                    by_token(pb[4 + m % 4], X0 + 4 * part, 4, a).then_inc(s["xv_T"], 1)

            def ssm_row(e):
                if e >= 2:
                    pe.wait_ge(s["e_ready"], e - 1)
                row(pb[4 + e % 2], MLH + e, NFD, gX).then_inc(s["bc_ready"], 1)

            for u in range(16):
                tile(HQ + u)
                if u == 1:
                    pe.wait_ge(s["xv_ev"], 2 * NT)
                    pe.wait_ge(s["conv_done"], 16 + 4)
                    for g in range(SSG):
                        for c, a, t, n in SC:
                            r = TT[a][1]
                            last = V.matmul(pb[4 + g][0:r, c:c + n], proj[:, B0 + g, TT[a][0]:TT[a][0] + r],
                                            proj[:, C0 + g, t:t + n], start=True, stop=True)
                        last.then_inc(s["cb_ready"], 1)
                if u == 2:
                    pe.wait_ge(s["cb_ev"], 1)
                    ssm_row(0)
                    ssm_row(1)
                for e in HEADS_AT[u]:
                    pe.wait_ge(s["pt_ready"], e + 1)
                    if e >= 4 and e % 2 == 0:
                        pe.wait_ge(s["y_ev"], e // 2 - 1)
                    q = 64 * (e % 2)
                    causal(pb[6 + (e // 2) % 2][q:q + 64, :],
                           lambda a, r: xv[0:r, a, e * 64:(e + 1) * 64],
                           lambda r, c, n: P2[0:r, e % 2, c:c + n]).then_inc(s["y_ready"], 1)
                    if e + 2 < SSH:
                        ssm_row(e + 2)

            norm_no = [0]

            def norm_sums(sq, groups, tiles, banks):
                pe.wait_ge(s["sq_ready"], norm_no[0] + 1)
                for g in range(groups):
                    product(pb[banks + g][:, 0:T],
                            [(ones[:, 0:P], sq[:, g * tiles + j, :]) for j in range(tiles)]).then_inc(s["sum_ready"], 1)
                norm_no[0] += 1

            tile(MQ)
            tile(MQ + 1)
            norm_sums(sq8, 4, 2, 4)
            tile(MQ + 2)

            def v_by_token(c):
                if c:
                    pe.wait_ge(s["hv_ev"], c)
                by_token(pb[7], (HV, MV)[c // 3], 4, c % 3).then_inc(s["hv_T"], 1)

            pe.wait_ge(s["rs_ready"], 1)
            for c in range(3):
                v_by_token(c)

            def level(l):
                if l < 0:
                    pe.wait_ge(s["hlin"], 1)
                else:
                    pe.wait_ge(s["lv_w"], l + 1)
                    pe.wait_ge(s["lv_ev"], l + 1)
                b = 4
                ks = proj[:, HF:HF + 4, :] if l < 0 else W[l % 2]
                qs = proj[:, HQ:HQ + 4, :] if l < 0 else W[l % 2]
                for h in range(HGH):
                    if l < 7:
                        for a in range(2):
                            last = V.matmul(pb[b + a][:, h * P:(h + 1) * P], ks[:, h, a * P:(a + 1) * P],
                                            qs[:, h, a * P:(a + 1) * P], start=True, stop=True)
                        if l < 0 or LH[l] <= 8:
                            last = V.matmul(pb[b + 2][0:TL, h * TL:(h + 1) * TL], ks[:, h, 2 * P:T],
                                            qs[:, h, 2 * P:T], start=True, stop=True)
                    elif l == 7:
                        last = V.matmul(pb[b][:, h * P:(h + 1) * P], ks[:, h, 0:P], qs[:, h, P:2 * P],
                                        start=True, stop=True)
                    else:
                        for a in range(2):
                            last = V.matmul(pb[b][:, (4 * a + h) * TL:(4 * a + h + 1) * TL],
                                            ks[:, h, a * P:(a + 1) * P], qs[:, h, 2 * P:T],
                                            start=True, stop=True)
                last.then_inc(s["lvd_ps"] if l < 0 else s["lv_ps"], 1)

            for u in range(5):
                tile(MQ + 3 + u)
                for l in LEVELS_AT[u]:
                    level(l)
            pe.wait_ge(s["in_ev"], MV + 4 + 4)
            for c in range(3, 6):
                v_by_token(c)
            pe.wait_ge(s["lv_ev"], NLEV + 1)
            for h in range(HGH):
                if h >= 2:
                    pe.wait_ge(s["ho_ev"], h - 1)
                causal(pb[4 + h % 2], lambda a, r: hv[0:r, a, h * P:(h + 1) * P],
                       lambda r, c, n: PHs[0:r, h, c:c + n]).then_inc(s["ho_ps"], 1)

            for h in range(MLH):
                q = 64 * (h % 2)
                if h == 0:
                    pe.wait_ge(s["ho_ev"], HGH)
                    pe.wait_ge(s["hv_ev"], 2 * NT)
                else:
                    pe.wait_ge(s["ml_h"], h)
                for c, a, t, n in SC:
                    r = TT[a][1]
                    last = V.matmul(pb[4][0:r, c:c + n], proj[q:q + 64, MK + h // 2, TT[a][0]:TT[a][0] + r],
                                    proj[q:q + 64, MQ + h // 2, t:t + n], start=True, stop=True)
                row(pb[5], h, MLH, gG).then_inc(s["ml_ps"], 1)
                tile(MO + h)
                pe.wait_ge(s["ml_e"], h + 1)
                row(pb[5], h, MLH, gZ)
                pe.wait_ge(s["ml_pt"], h + 1)
                causal(pb[6], lambda a, r: mv[0:r, a, h * P:(h + 1) * P],
                       lambda r, c, n: P2[0:r, h % 2, c:c + n])
                causal(pb[7], lambda a, r: ones[0:r, 0:P],
                       lambda r, c, n: P2[0:r, h % 2, c:c + n]).then_inc(s["ml_o"], 1)
            pe.wait_ge(s["ml_h"], MLH)
            norm_sums(sqH, 4, 1, 4)
            norm_sums(sqH, 4, 1, 4)

            pe.wait_ge(s["norm_done"], 1)
            for j in (0, 1, 2, 4):
                pe.sem_inc(m_free[j], 1)
            pe.sem_inc(s["h_ps"], 1)
            pe.sem_inc(s["y_ps"], 1)
            project(4, 13, lambda k: proj[:, MIXED[k], :])

            pe.wait_ge(s["routerw_in"], 80)
            for k in range(KD):
                pe.wait_ge(s["u2T_ready"], k + 1)
                last = V.matmul(pb[4][0:LG, 0:T], wr[:, k, :], uT[:, k, :], start=k == 0, stop=k == KD - 1)
            last.then_inc(s["lg_ready"], 1)
            pe.wait_ge(s["sq_acc"], KD + 1)
            for a, (t, n) in enumerate(TT):
                last = V.matmul(pb[6][0:n, a:a + 1], sqa[:, t:t + n], ones[:, 0:1], start=True, stop=True)
            last.then_inc(s["sum2"], 1)
            pe.wait_ge(s["lg_ev"], 1)
            for a, (t, n) in enumerate(TT):
                last = V.transpose(pb[5][0:n, a * LG:(a + 1) * LG], lgT[0:LG, t:t + n], ident[0:LG, 0:LG])
            last.then_inc(s["lg_T"], 1)
            for a, (t, n) in enumerate(TT):
                for q in range(4):
                    if a >= 1:
                        pe.wait_ge(s["t_ev"], 4 * a + q - 3)
                    for j in range(4):
                        last = V.transpose(pb[q][0:n, j * P:(j + 1) * P], uT[:, 4 * q + j, t:t + n], ident[:, :])
                    last.then_inc(s["t_ps"], 1)
            pe.wait_ge(s["pairs"], 1)
            for a, (t, n) in enumerate(TT):
                product(pb[6][0:n, a * NE:(a + 1) * NE],
                        [(ones[:, 0:n], chosen[:, j, :]) for j in range(a)]
                        + [(before[0:n, 0:n], chosen[0:n, a, :])])
            product(pb[6][:, NT * NE:(NT + 1) * NE],
                    [(ones[0:n, 0:P], chosen[0:n, a, :]) for a, (t, n) in enumerate(TT)]).then_inc(s["ranks"], 1)
            for m in range(2 * NT):
                n = TT[m // 2][1]
                pe.wait_ge(s["rhs_ready"], m + 1)
                last = V.matmul(pb[7][:, 0:3 * NC_], slot_hot[m % 2][0:n, :],
                                rhs_t[m % 2][0:n, :, :].rearrange("p a c -> p (a c)"),
                                start=m == 0, stop=m == 2 * NT - 1)
                last.then_inc(s["rhs_used"], 1)
            pe.wait_ge(s["t_ev"], 12)
            pe.wait_ge(s["idx_ready"], 1)
            for tb in range(2):
                for q in range(4):
                    for j in range(4):
                        last = V.transpose(pb[4 * tb + q][:, j * P:(j + 1) * P],
                                           hT[:, 4 * q + j, NM + tb * P:NM + (tb + 1) * P], ident[:, :])
                    last.then_inc(s["h2_ps"], 1)
            pe.wait_ge(s["h2_ev"], 8)

            def expert(n, landed_rows):
                pe.wait_ge(s["xs_in"], landed_rows)
                for c in range(8):
                    last = V.transpose(pb[c // 4][:, (c % 4) * P:(c % 4 + 1) * P], xs[:, c * P:(c + 1) * P],
                                       ident[:, :])
                last.then_inc(s["xT_ps"], 1)
                pe.wait_ge(s["xT_ev"], n + 1)
                pe.wait_ge(s["xT_ev2"], n + 1)
                for part in range(2):
                    pe.wait_ge(m_in[2 * part], n * 16 + 16)
                    pe.wait_ge(m_in[2 * part + 1], n * 16 + 16)
                    for c in range(8):
                        for g in range(2):
                            w = slot((2 * part + g + 2) % 6).rearrange("p (k f) -> p k f", f=FE)
                            last = V.matmul(pb[2][64 * g:64 * g + 64, :], xsT[:, c, part, :], w[:, c, :],
                                            start=part + c == 0, stop=part == 1 and c == 7)
                            if c == 7:
                                last.then_inc(s["h_ps"] if part and g else m_free[2 * part + g], 1)
                pe.wait_ge(s["h_ev"], n + 1)
                for k in range(KF):
                    last = V.transpose(pb[3][:, k * P:(k + 1) * P], hs[:, k * P:(k + 1) * P], ident[:, :])
                last.then_inc(s["hT_ps"], 1)
                pe.wait_ge(s["hT_ready"], n + 1)
                pe.wait_ge(s["y_free"], n + 1)
                for k in range(KF):
                    if k % 2 == 0:
                        pe.wait_ge(m_in[4 + k // 2], n * 16 + 16)
                    w = slot(k // 2).rearrange("p (k d) -> p k d", d=D)
                    for d in range(2):
                        for g in range(2):
                            last = V.matmul(pb[4 + d][64 * g:64 * g + 64, :], hTb[:, k, :],
                                            w[:, k % 2, g * 1024 + d * 512:g * 1024 + (d + 1) * 512],
                                            start=k == 0, stop=k == KF - 1)
                    if k == 1:
                        last.then_inc(m_free[4], 1)
                last.then_inc(s["y_ps"], 1)

            with pe.Fori(0, NE) as i:
                expert(i, i * 16 + 16)
            pe.wait_ge(s["ov_ready"], 1)
            count = pe.value_load(ov_n[0:1, 0:1], min_val=0, max_val=NOV)
            with pe.If(count > 0):
                with pe.Fori(0, count) as i:
                    expert(i + NE, i * 16 + (NE + 2) * 16)


_INS = ['x', 'meta_tokens', 'hg_lb_logits', 'norm_mix_w', 'w_in', 'hg_norm_w', 'ml_b_i', 'ml_b_f', 'ml_norm_w',
        'ssm_conv_w', 'ssm_conv_b', 'ssm_dt_bias', 'ssm_a_log', 'ssm_d', 'ssm_norm_w', 'w_out', 'norm_ffn_w',
        'moe_w_group', 'moe_b_group', 'moe_w_router', 'moe_b_router', 'moe_w1', 'moe_w3', 'moe_w2', 'final_norm_w']
_OUTS = [((1, 256, 2048), 'float32')]


def kernel(**inputs):
    import numpy as _np
    import concourse.bacc as _bacc
    from concourse import mybir as _mybir
    from concourse.bass_utils import run_bass_kernel_spmd as _run

    nc = _bacc.Bacc("TRN2", target_bir_lowering=False, num_devices=1)
    arrays, args = {}, []
    for name in _INS:
        a = _np.ascontiguousarray(inputs[name])
        arrays[f"in_{name}_dram"] = a
        args.append(nc.dram_tensor(f"in_{name}_dram", a.shape, _mybir.dt.from_np(a.dtype), kind="ExternalInput").ap())
    for i, (shape, dtype) in enumerate(_OUTS):
        dt = _mybir.dt.from_np(_np.dtype(dtype))
        args.append(nc.dram_tensor(f"out_{i}_dram", shape, dt, kind="ExternalOutput").ap())
    hymba_moe_layer(nc, *args)
    r = _run(nc, [arrays], core_ids=[0])
    return r.results[0]["out_0_dram"]
```
